# Optimizing a Trainium2 kernel written in Bass

```python
import math
import jax, jax.numpy as jnp
from jax import lax
import numpy as np

D_MODEL = 2048
BATCH = 1
SEQ = 512
DEPTH = 1

CHUNK = 64
MIX_WIDTH = D_MODEL
GDN_DK = 128
GDN_DV = 128
GDN_HEADS = (MIX_WIDTH // 2) // GDN_DV
CONV_WIDTH = 4
SWA_HEAD_DIM = 64
SWA_Q_HEADS = (MIX_WIDTH // 2) // SWA_HEAD_DIM
SWA_KV_HEADS = SWA_Q_HEADS // 4
SWA_WINDOW = 128
SWA_WINDOW_CHUNKS = SWA_WINDOW // CHUNK
MOE_GROUPS = 4
EXPERTS_PER_GROUP = 8
N_EXPERTS = MOE_GROUPS * EXPERTS_PER_GROUP
TOP_K = 2
D_EXPERT = 512
MOE_BLOCK = 128
ALPHA = (2.0 * DEPTH) ** 0.25
BETA_INIT = (8.0 * DEPTH) ** -0.25
LN_EPS = 1e-5
RMS_EPS = 1e-6

A_QK = GDN_HEADS * GDN_DK
A_V = GDN_HEADS * GDN_DV
A_QKV = 2 * A_QK + A_V
B_Q = SWA_Q_HEADS * SWA_HEAD_DIM
B_KV = SWA_KV_HEADS * SWA_HEAD_DIM
COL_SIZES = [A_QKV, A_V, GDN_HEADS, GDN_HEADS, B_Q, B_KV, B_KV]
SPLITS = [int(s) for s in np.cumsum(COL_SIZES)[:-1]]
IN_COLS = int(sum(COL_SIZES))

kernel_name = "hymba_gdn_swa_sink_alibi_hmoe_deepnorm"

def layer_norm(x, g, b):
    xf = x.astype(jnp.float32)
    mu = jnp.mean(xf, -1, keepdims=True)
    var = jnp.mean(jnp.square(xf - mu), -1, keepdims=True)
    return ((xf - mu) * lax.rsqrt(var + LN_EPS) * g.astype(jnp.float32) + b.astype(jnp.float32)).astype(x.dtype)

def l2norm(t):
    return t * lax.rsqrt(jnp.sum(t * t, -1, keepdims=True) + RMS_EPS)

def causal_conv(x, w):
    K = w.shape[0]
    S = x.shape[1]
    xp = jnp.pad(x, ((0, 0), (K - 1, 0), (0, 0)))
    return sum(xp[:, j:j + S] * w[j] for j in range(K))

def alibi_slopes(n_heads):
    h = jnp.arange(1, n_heads + 1, dtype=jnp.float32)
    return jnp.exp2(-8.0 * h / n_heads)

def gated_delta_rule(q, k, v, g, beta):
    B, S, H, dk = q.shape
    dv = v.shape[-1]
    NC = S // CHUNK
    f32 = jnp.float32
    q = l2norm(q.astype(f32)) * (dk ** -0.5)
    k = l2norm(k.astype(f32))
    v = v.astype(f32)

    def to_chunks(t):
        return t.reshape(B, NC, CHUNK, H, -1).transpose(1, 0, 3, 2, 4)

    def to_chunks_s(t):
        return t.reshape(B, NC, CHUNK, H).transpose(1, 0, 3, 2)

    qc, kc, vc = to_chunks(q), to_chunks(k), to_chunks(v)
    gc = jnp.cumsum(to_chunks_s(g.astype(f32)), -1)
    bc = to_chunks_s(beta.astype(f32))
    tril = jnp.tril(jnp.ones((CHUNK, CHUNK), bool))
    strict = jnp.tril(jnp.ones((CHUNK, CHUNK), bool), -1)
    decay = jnp.exp(jnp.where(tril, gc[..., :, None] - gc[..., None, :], -jnp.inf))
    kb = kc * bc[..., None]
    vb = vc * bc[..., None]
    L = jnp.where(strict, jnp.einsum('nbhik,nbhjk->nbhij', kb, kc) * decay, 0.0)
    eye = jnp.eye(CHUNK, dtype=f32)
    rhs = jnp.concatenate([vb, kb * jnp.exp(gc)[..., None]], -1)
    sol = lax.linalg.triangular_solve(L + eye, rhs, left_side=True, lower=True, unit_diagonal=True)
    u, w = sol[..., :dv], sol[..., dv:]
    attn = jnp.einsum('nbhik,nbhjk->nbhij', qc, kc) * decay
    q_dec = qc * jnp.exp(gc)[..., None]
    k_dec = kc * jnp.exp(gc[..., -1:] - gc)[..., None]
    chunk_decay = jnp.exp(gc[..., -1])

    def step(state, inp):
        qd, kd, uu, ww, at, cd = inp
        v_new = uu - jnp.einsum('bhck,bhkv->bhcv', ww, state)
        o = jnp.einsum('bhck,bhkv->bhcv', qd, state) + jnp.einsum('bhij,bhjv->bhiv', at, v_new)
        state = state * cd[..., None, None] + jnp.einsum('bhck,bhcv->bhkv', kd, v_new)
        return state, o

    s0 = jnp.zeros((B, H, dk, dv), f32)
    _, o = lax.scan(step, s0, (q_dec, k_dec, u, w, attn, chunk_decay))
    return o.transpose(1, 0, 3, 2, 4).reshape(B, S, H, dv)

def sliding_window_sink_attention(q, k, v, sinks):
    B, S, Hq, d = q.shape
    Hkv = k.shape[2]
    G = Hq // Hkv
    NC = S // CHUNK
    W = SWA_WINDOW_CHUNKS
    qc = q.reshape(B, NC, CHUNK, Hkv, G, d)

    def band(t):
        tc = t.reshape(B, NC, CHUNK, Hkv, d)
        tp = jnp.pad(tc, ((0, 0), (W - 1, 0), (0, 0), (0, 0), (0, 0)))
        return jnp.concatenate([tp[:, j:j + NC] for j in range(W)], axis=2)

    kb, vb = band(k), band(v)
    kk = jnp.arange(W * CHUNK)
    qi = jnp.arange(CHUNK)
    n = jnp.arange(NC)
    valid = (n[:, None, None] - (W - 1) + kk[None, None, :] // CHUNK) >= 0
    dist = jnp.abs(qi[:, None] + (W - 1) * CHUNK - kk[None, :]).astype(jnp.float32)
    slopes = alibi_slopes(Hq).reshape(Hkv, G)
    s = jnp.einsum('bnqhgd,bnkhd->bhgnqk', qc, kb).astype(jnp.float32) * (d ** -0.5)
    s = s - slopes[:, :, None, None, None] * dist
    s = jnp.where(valid, s, -jnp.inf)
    sink = jnp.broadcast_to(sinks.astype(jnp.float32).reshape(Hkv, G)[None, :, :, None, None, None], s.shape[:-1] + (1,))
    p = jax.nn.softmax(jnp.concatenate([s, sink], -1), axis=-1)[..., :-1]
    o = jnp.einsum('bhgnqk,bnkhd->bnqhgd', p.astype(v.dtype), vb)
    return o.reshape(B, S, Hq * d)

def token_mixer(x, w_in, conv_w, a_log, dt_bias, gdn_norm_w, sinks, w_o):
    B, S, _ = x.shape
    h = x @ w_in
    a_qkv, a_z, a_beta, a_dec, b_q, b_k, b_v = jnp.split(h, SPLITS, axis=-1)
    a_qkv = jax.nn.silu(causal_conv(a_qkv, conv_w))
    a_q, a_k, a_v = jnp.split(a_qkv, [A_QK, 2 * A_QK], axis=-1)
    a_q = a_q.reshape(B, S, GDN_HEADS, GDN_DK)
    a_k = a_k.reshape(B, S, GDN_HEADS, GDN_DK)
    a_v = a_v.reshape(B, S, GDN_HEADS, GDN_DV)
    beta = jax.nn.sigmoid(a_beta.astype(jnp.float32))
    g = -jnp.exp(a_log.astype(jnp.float32)) * jax.nn.softplus(a_dec.astype(jnp.float32) + dt_bias.astype(jnp.float32))
    o_a = gated_delta_rule(a_q, a_k, a_v, g, beta)
    z = a_z.reshape(B, S, GDN_HEADS, GDN_DV).astype(jnp.float32)
    o_a = o_a * lax.rsqrt(jnp.mean(o_a * o_a, -1, keepdims=True) + RMS_EPS) * gdn_norm_w.astype(jnp.float32) * jax.nn.silu(z)
    o_a = o_a.reshape(B, S, A_V).astype(x.dtype)
    o_b = sliding_window_sink_attention(
        b_q.reshape(B, S, SWA_Q_HEADS, SWA_HEAD_DIM),
        b_k.reshape(B, S, SWA_KV_HEADS, SWA_HEAD_DIM),
        b_v.reshape(B, S, SWA_KV_HEADS, SWA_HEAD_DIM), sinks)
    return jnp.concatenate([o_a, o_b.astype(x.dtype)], -1) @ w_o

def hierarchical_moe(x, w_route_group, w_route_expert, w_gate, w_up, w_down):
    B, S, D = x.shape
    T = B * S
    xt = x.reshape(T, D)
    glog = (xt @ w_route_group).astype(jnp.float32)
    gprob = jax.nn.softmax(glog, -1)
    g_sel = jnp.argmax(glog, -1)
    p_g = jnp.take_along_axis(gprob, g_sel[:, None], -1)
    elog = (xt @ w_route_expert).astype(jnp.float32).reshape(T, MOE_GROUPS, EXPERTS_PER_GROUP)
    elog = jnp.take_along_axis(elog, g_sel[:, None, None], axis=1)[:, 0]
    top_p, top_i = lax.top_k(jax.nn.softmax(elog, -1), TOP_K)
    weights = p_g * top_p / jnp.sum(top_p, -1, keepdims=True)
    eid = g_sel[:, None].astype(jnp.int32) * EXPERTS_PER_GROUP + top_i.astype(jnp.int32)
    A = T * TOP_K
    e_flat = eid.reshape(A)
    w_flat = weights.reshape(A)
    tok_flat = jnp.arange(A, dtype=jnp.int32) // TOP_K
    order = jnp.argsort(e_flat)
    e_sorted, tok_sorted, w_sorted = e_flat[order], tok_flat[order], w_flat[order]
    counts = jnp.bincount(e_flat, length=N_EXPERTS)
    padded = (counts + MOE_BLOCK - 1) // MOE_BLOCK * MOE_BLOCK
    start = jnp.cumsum(counts) - counts
    pend = jnp.cumsum(padded)
    pstart = pend - padded
    dest = pstart[e_sorted] + (jnp.arange(A, dtype=jnp.int32) - start[e_sorted])
    NB = A // MOE_BLOCK + N_EXPERTS
    P = NB * MOE_BLOCK
    row_tok = jnp.zeros((P,), jnp.int32).at[dest].set(tok_sorted)
    row_w = jnp.zeros((P,), jnp.float32).at[dest].set(w_sorted)
    blk_e = jnp.minimum(jnp.searchsorted(pend, jnp.arange(NB) * MOE_BLOCK, side='right'), N_EXPERTS - 1)
    xb = xt[row_tok].reshape(NB, MOE_BLOCK, D)

    def expert_block(args):
        xblk, e = args
        hdn = jax.nn.silu(xblk @ w_gate[e]) * (xblk @ w_up[e])
        return hdn @ w_down[e]

    yb = lax.map(expert_block, (xb, blk_e)).reshape(P, D)
    y = jax.ops.segment_sum(yb * row_w[:, None].astype(yb.dtype), row_tok, num_segments=T)
    return y.reshape(B, S, D)

def setup_inputs(seed: int = 0) -> dict:
    key = jax.random.key(seed)
    ks = jax.random.split(key, 20)
    D = D_MODEL
    f32 = jnp.float32
    x = jax.random.normal(ks[0], (BATCH, SEQ, D), f32)
    ln0_g = 1.0 + 0.02 * jax.random.normal(ks[1], (D,), f32)
    ln0_b = 0.02 * jax.random.normal(ks[2], (D,), f32)
    col_scale = np.ones((IN_COLS,), np.float32)
    col_scale[2 * A_QK:A_QKV] = BETA_INIT
    col_scale[IN_COLS - B_KV:] = BETA_INIT
    w_in = jax.random.normal(ks[3], (DEPTH, D, IN_COLS), f32) * (D ** -0.5) * jnp.asarray(col_scale)
    conv_w = 0.5 * jax.random.normal(ks[4], (DEPTH, CONV_WIDTH, A_QKV), f32)
    a_log = jnp.log(jax.random.uniform(ks[5], (DEPTH, GDN_HEADS), f32, 1.0, 16.0))
    dt = jnp.exp(jax.random.uniform(ks[6], (DEPTH, GDN_HEADS), f32, math.log(1e-3), math.log(1e-1)))
    dt_bias = dt + jnp.log(-jnp.expm1(-dt))
    gdn_norm_w = 1.0 + 0.02 * jax.random.normal(ks[7], (DEPTH, GDN_DV), f32)
    sinks = 0.5 * jax.random.normal(ks[8], (DEPTH, SWA_Q_HEADS), f32)
    w_o = jax.random.normal(ks[9], (DEPTH, MIX_WIDTH, D), f32) * (MIX_WIDTH ** -0.5) * BETA_INIT
    ln1_g = 1.0 + 0.02 * jax.random.normal(ks[10], (DEPTH, D), f32)
    ln1_b = 0.02 * jax.random.normal(ks[11], (DEPTH, D), f32)
    w_route_group = jax.random.normal(ks[12], (DEPTH, D, MOE_GROUPS), f32) * (D ** -0.5)
    w_route_expert = jax.random.normal(ks[13], (DEPTH, D, N_EXPERTS), f32) * (D ** -0.5)
    w_gate = jax.random.normal(ks[14], (DEPTH, N_EXPERTS, D, D_EXPERT), f32) * (D ** -0.5)
    w_up = jax.random.normal(ks[15], (DEPTH, N_EXPERTS, D, D_EXPERT), f32) * (D ** -0.5)
    w_down = jax.random.normal(ks[16], (DEPTH, N_EXPERTS, D_EXPERT, D), f32) * (D_EXPERT ** -0.5) * BETA_INIT
    ln2_g = 1.0 + 0.02 * jax.random.normal(ks[17], (DEPTH, D), f32)
    ln2_b = 0.02 * jax.random.normal(ks[18], (DEPTH, D), f32)
    return {"x": x, "ln0_g": ln0_g, "ln0_b": ln0_b, "w_in": w_in, "conv_w": conv_w,
            "a_log": a_log, "dt_bias": dt_bias, "gdn_norm_w": gdn_norm_w, "sinks": sinks,
            "w_o": w_o, "ln1_g": ln1_g, "ln1_b": ln1_b, "w_route_group": w_route_group,
            "w_route_expert": w_route_expert, "w_gate": w_gate, "w_up": w_up, "w_down": w_down,
            "ln2_g": ln2_g, "ln2_b": ln2_b}

def reference(x, ln0_g, ln0_b, w_in, conv_w, a_log, dt_bias, gdn_norm_w, sinks, w_o,
              ln1_g, ln1_b, w_route_group, w_route_expert, w_gate, w_up, w_down, ln2_g, ln2_b):
    h = layer_norm(x, ln0_g, ln0_b)
    for l in range(DEPTH):
        mix = token_mixer(h, w_in[l], conv_w[l], a_log[l], dt_bias[l], gdn_norm_w[l], sinks[l], w_o[l])
        h = layer_norm(ALPHA * h + mix, ln1_g[l], ln1_b[l])
        ffn = hierarchical_moe(h, w_route_group[l], w_route_expert[l], w_gate[l], w_up[l], w_down[l])
        h = layer_norm(ALPHA * h + ffn, ln2_g[l], ln2_b[l])
    return h


_drawn_inputs = setup_inputs


def setup_inputs(seed=0):
    import zlib

    import numpy as np

    out = dict(_drawn_inputs(seed))
    spreads = {}
    factors = {'gdn_norm_w': 7.385, 'sinks': 8.0, 'ln2_g': 2.823, 'ln2_b': 2.842}
    for name, (base, spread) in spreads.items():
        noise = np.random.default_rng([zlib.crc32(name.encode()), seed]).standard_normal(out[name].shape)
        drawn = base * np.exp(spread * noise) if base else spread * noise
        out[name] = __import__('jax').numpy.asarray(drawn.astype(out[name].dtype))
    for name, factor in factors.items():
        out[name] = (out[name] * factor).astype(out[name].dtype)
    return out
```

```python
from contextlib import ExitStack

import numpy as np

import concourse.bass as bass
from concourse import mybir

ALU = mybir.AluOpType
ACT = mybir.ActivationFunctionType
F32 = mybir.dt.float32
F32R = mybir.dt.float32r
I32 = mybir.dt.int32
AX = mybir.AxisListType

P = 128
D = 2048
S = 512
TT = S // P
KD = D // P
HEADS = 8
DK = 128
CONV = 4
QH, KVH, HD = 16, 4, 64
CHUNK = 64
A_QKV = 3 * HEADS * DK
C_BETA = 4 * HEADS * DK
C_BQ = C_BETA + 2 * HEADS
C_BK = C_BQ + QH * HD
C_BV = C_BK + KVH * HD
IN_COLS = C_BV + KVH * HD
GROUPS, PER_GROUP = 4, 8
E = GROUPS * PER_GROUP
F = 512
KF = F // P
SLOTS = 64
CAP = S
LEFTOVER = S * 2 // SLOTS
ALPHA = 2.0 ** 0.25
LN_EPS, RMS_EPS = 1e-5, 1e-6
NEG = -1.0e30

STRIPS = 1 + 4 * (HEADS + 1) + 8
PIECES = 16
LEVELS = 6

K_ID = 0
K_TRI = K_ID + P
K_ONE = K_TRI + P
K_M1T = K_ONE + P
K_MASK = K_M1T + P
K_END = K_MASK + 7 * P
J_DIST = 0
J_SLOPE = J_DIST + 3 * 2 * P
J_END = J_SLOPE + QH


def shape_constants():
    i = np.arange(P)[:, None]
    j = np.arange(P)[None, :]
    k = np.zeros((P, K_END), np.float32)
    k[:, K_ID:K_ID + P] = i == j
    k[:, K_TRI:K_TRI + P] = i <= j
    k[:, K_ONE:K_ONE + P] = 1.0
    for l in range(7):
        b = 1 << l
        m = (i // (2 * b) == j // (2 * b)) & (i % (2 * b) >= b) & (j % (2 * b) < b)
        k[:, K_MASK + l * P:K_MASK + (l + 1) * P] = m
        if l == 0:
            k[:, K_M1T:K_M1T + P] = m.T
    a = np.zeros((P, J_END), np.float32)
    key = np.arange(2 * P)[None, :] - P
    seen = (key // CHUNK >= i // CHUNK - 1) & (key // CHUNK <= i // CHUNK)
    dist = np.where(seen, np.abs(i - key), -NEG).astype(np.float32)
    first = np.where(key >= 0, dist, np.float32(-NEG))
    a[:, 0:2 * P] = first
    a[:, 2 * P:4 * P] = dist
    a[:, 4 * P:6 * P] = dist
    a[:, J_SLOPE:J_END] = -(2.0 ** (-8.0 * np.arange(1, QH + 1) / QH))[None, :]
    r = np.zeros((P, 3 * E + TT + S), np.float32)
    r[:, 0:E] = np.arange(E)[None, :]
    r[:, E:2 * E] = (np.arange(E) * CAP)[None, :]
    r[:, 2 * E:3 * E] = np.arange(E)[None, :] // PER_GROUP
    r[:, 3 * E:3 * E + TT] = np.arange(TT)[None, :] * P + i
    r[:, 3 * E + TT:] = np.arange(S)[None, :]
    return k, a, r


def build(nc, x, ln0_g, ln0_b, w_in, conv_w, a_log, dt_bias, gdn_norm_w, sinks, w_o, ln1_g, ln1_b,
          w_route_group, w_route_expert, w_gate, w_up, w_down, ln2_g, ln2_b, consts, att_consts,
          route_consts, out):
    x2 = x[0].rearrange("(t p) d -> p t d", p=P)
    out2 = out[0].rearrange("(t p) d -> p t d", p=P)
    w_in_v = w_in[0].rearrange("(k p) n -> p k n", p=P)
    w_o_v = w_o[0].rearrange("(k p) n -> p k n", p=P)
    gate_v = w_gate[0].rearrange("e (k p) f -> p e k f", p=P)
    up_v = w_up[0].rearrange("e (k p) f -> p e k f", p=P)
    down_v = w_down[0].rearrange("e (c p) n -> p e c n", p=P)

    ctx = ExitStack()
    with ctx:
        def sem(name):
            return ctx.enter_context(nc.semaphore(name))

        def dram(name, shape, dt):
            return nc.dram_tensor(name, shape, dt).ap()

        h_scr = dram("h_scr", (S, D), F32)
        h1_scr = dram("h1_scr", (S, D), F32)
        slot_rows = dram("slot_rows", (E * CAP, 2), I32)
        h_scr_v = h_scr.rearrange("(t p) d -> p t d", p=P)
        h1_scr_v = h1_scr.rearrange("(t p) d -> p t d", p=P)

        ARENA = 212000
        arena = ctx.enter_context(nc.sbuf_tensor("arena", [P, ARENA // 4], F32))
        base = nc.sbuf_base - ARENA
        placed = {}

        def at(name, offset, shape, dt=F32):
            size = 4 * int(np.prod(shape[1:]))
            assert offset + size <= ARENA, (name, offset + size)
            placed[name] = offset + size
            return nc.alloc_sbuf_tensor_at(name, list(shape), dt, offset=base + offset)

        KB = 1024
        HT, ST, MX, GD, CN = 0, 64 * KB, 112 * KB, 144 * KB, 198 * KB
        hTh = at("hTh", HT, [P, KD, S], F32R)
        hTl = at("hTl", HT + 32 * KB, [P, KD, S], F32R)
        raw = [at(f"raw{i}", ST + 8 * KB * i, [P, KD * P]) for i in range(2)]
        whi = [at(f"whi{i}", ST + 8 * KB * (2 + i), [P, KD, P], F32R) for i in range(2)]
        wlo = [at(f"wlo{i}", ST + 8 * KB * (4 + i), [P, KD, P], F32R) for i in range(2)]
        mixT = at("mixT", MX, [P, KD, S])
        xt = [at(f"xt{i}", GD + 8 * KB * i, [P, D]) for i in range(2)]
        xn = [at(f"xn{i}", GD + 8 * KB * (2 + i), [P, D]) for i in range(2)]
        g0 = at("g0", GD + 32 * KB, [P, D])
        b0 = at("b0", GD + 40 * KB, [P, D])
        o = GD
        xp = [at(f"xp{j}", o + 2112 * j, [P, S + CONV]) for j in range(3)]
        o += 2112 * 3
        half = [at(f"half{j}", o + 2 * KB * j, [P, S]) for j in range(4)]
        o += 8 * KB
        th = [at(f"th{j}", o + 2 * KB * j, [P, S]) for j in range(4)]
        o += 8 * KB
        ATT = o
        names = ["q", "k", "v", "dm", "L", "X", "XT", "qd", "Ed", "LT", "attnT", "vb", "kd", "A", "sz"]
        T = {}
        for n in names:
            T[n] = at("gd_" + n, o, [P, S])
            o += 2 * KB
        vn = at("vn", o, [P, P]); o += 512
        rr = at("rr", o, [P, P]); o += 512
        st = at("st", o, [P, P]); o += 512
        assert o <= CN, o
        kdup = at("kdup", GD, [P, KVH, S + P])
        vT = at("vT", GD + 10 * KB, [P, 2, S])
        vtok = at("vtok", GD + 14 * KB, [P, TT, KVH * HD])
        dist = at("dist", GD + 18 * KB, [P, 3, 2 * P])
        aq = [at(f"aq{i}", ATT + 2 * KB * i, [P, S]) for i in range(4)]
        sc = at("sc", ATT + 8 * KB, [P, 2, 2, 2, 2 * P])
        pT = at("pT", ATT + 16 * KB, [P, 4, S])
        kg = at("kg", ATT + 24 * KB, [P, S + P])
        vg = at("vg", ATT + 24 * KB + 2560, [P, TT, HD])
        sl = at("sl", ATT + 24 * KB + 2560 + 1024, [P, 2, 4])
        mxh = at("mxh", HT, [P, KD, S], F32R)
        mxl = at("mxl", HT + 32 * KB, [P, KD, S], F32R)
        r1 = at("r1", MX, [P, TT, D])
        g1 = at("g1", GD, [P, D])
        b1 = at("b1", GD + 8 * KB, [P, D])
        h1T = at("h1T", GD + 16 * KB, [P, KD, S])
        wr = at("wr", GD + 48 * KB, [P, KD, GROUPS + E])
        wpiece = [at(f"wpiece{i}", HT + 8 * KB * i, [P, 4 * F]) for i in range(12)]
        xb = at("xb", GD + 16 * KB, [SLOTS, D])
        yw = at("yw", GD + 24 * KB, [P, 4, F])
        yhl = at("yhl", GD + 32 * KB, [P, 4, F], F32R)
        xbT = at("xbT", GD + 40 * KB, [P, KD, SLOTS])
        hid = at("hid", GD + 48 * KB, [P, F])
        hidT = at("hidT", GD + 44 * KB, [P, KF, SLOTS])
        place = at("place", GD + 45 * KB, [P, S], F32R)
        tokens = at("tokens", GD + 51 * KB, [P, S])
        g2 = at("g2", HT + 96 * KB, [P, D])
        b2 = at("b2", HT + 104 * KB, [P, D])
        o = CN
        small = {}

        def keep(name, shape, dt=F32):
            nonlocal o
            t = at(name, o, shape, dt)
            o += (4 * int(np.prod(shape[1:])) + 31) // 32 * 32
            return t

        cst = keep("cst", [P, K_END])
        rc = keep("rc", [P, 3 * E + TT])
        attn_small = keep("attn_small", [P, 2 * QH])
        cw = keep("cw", [P, CONV * 24])
        cwraw = at("cwraw", GD + 52 * KB, [CONV * 24, P])
        cwh = keep("cwh", [P, CONV, 3])
        eps = keep("eps", [P, 2])
        nrm = keep("nrm", [P, 1])
        bns = keep("bns", [P, 4, 6])
        bns4 = keep("bns4", [P, TT, 4, 6])
        mv = keep("mv", [P, 2])
        mv4 = keep("mv4", [P, TT, 2])
        rs4 = keep("rs4", [P, TT])
        nm4 = keep("nm4", [P, TT])
        rstd = keep("rstd", [P, 1])
        nmr = keep("nmr", [P, 1])
        tokpar = keep("tokpar", [P, HEADS, 6, TT])
        hp = keep("hp", [P, 6, TT])
        gb = at("gb", ATT + 2 * KB * names.index("A"), [P, TT, P])
        bd = at("bd", ATT, [P, S])
        ab = keep("ab", [P, 2, HEADS])
        bdt = at("bdt", ATT + 2 * KB * names.index("kd"), [P, TT, 2 * HEADS])
        att8 = keep("att8", [P, 5, 8])
        wk = at("wk", ATT + 2 * KB * names.index("vb"), [P, 6, TT, HEADS])
        slot_tw = keep("slot_tw", [P, 2])
        rd = keep("rd", [P, TT, 2], I32)
        idx = keep("idx", [P, 2], I32)
        ovi = keep("ovi", [1, 2 * LEFTOVER + 1], I32)
        o2_ = [GD]

        def scratch(name, shape, dt=F32):
            t = at(name, o2_[0], shape, dt)
            o2_[0] += (4 * int(np.prod(shape[1:])) + 31) // 32 * 32
            return t

        lg = scratch("lg", [P, TT, GROUPS + E])
        gm = scratch("gm", [P, 4, TT])
        ge = scratch("ge", [P, TT, GROUPS])
        gsel = scratch("gsel", [P, TT, E])
        el = scratch("el", [P, TT, E])
        top = scratch("top", [P, TT, 8])
        topi = scratch("topi", [P, TT, 8], mybir.dt.uint32)
        topf = scratch("topf", [P, TT, 2])
        oh = scratch("oh", [P, 2, TT, E])
        taken = scratch("taken", [P, TT, E])
        dstf = scratch("dstf", [P, TT, 2])
        wts = scratch("wts", [P, 4, TT])
        over_nb = scratch("over_nb", [P, 4, E])
        ovc = scratch("ovc", [1, LEFTOVER, E])
        ovp = scratch("ovp", [1, LEFTOVER, E])
        ovf = scratch("ovf", [1, 4, LEFTOVER])
        toki = scratch("toki", [P, TT, 2, 2], I32)
        assert o2_[0] <= GD + 16 * KB
        unused = at("unused", MX, [P, 2 * E * CAP // P], I32)
        ident = cst[:, K_ID:K_ID + P]
        tri = cst[:, K_TRI:K_TRI + P]
        ones = cst[:, K_ONE:K_ONE + P]

        banks = [ctx.enter_context(nc.psum_tensor(f"bank{i}", [P, S], F32)) for i in range(8)]
        PA = banks[0:2]
        B0, B1, B2, BM, BS, BO = banks[2:8]

        ld_const = sem("ld_const"); ld_small = sem("ld_small"); ld_x = [sem(f"ld_x{i}") for i in range(2)]
        ld_g0 = sem("ld_g0"); raw_loaded = [sem(f"raw_loaded{i}") for i in range(2)]
        ld_att = sem("ld_att")
        ln_step = sem("ln_step"); ln_sqrt = sem("ln_sqrt")
        ln_norm = sem("ln_norm")
        h_stored = [sem(f"h_stored{i}") for i in range(2)]
        hT_psum = sem("hT_psum"); hT_hi = sem("hT_hi"); hT_lo = sem("hT_lo")
        strip_hi = sem("strip_hi"); strip_lo = sem("strip_lo"); strip_mm = sem("strip_mm"); strip_out = sem("strip_out")

        zero_pad = sem("zero_pad"); cw_psum = sem("cw_psum"); cw_done = sem("cw_done")
        bd_T = sem("bd_T"); bd_done = sem("bd_done"); bda = sem("bda"); gcum = sem("gcum")
        par_done = sem("par_done")
        kpad = sem("kpad")
        taps = sem("taps")
        conv_w_ready = sem("conv_w_ready")
        tanh_done = sem("tanh_done")
        silu = [sem(f"silu{j}") for j in range(4)]
        hp_ready = sem("hp_ready"); gb_ready = sem("gb_ready")
        sq_done = sem("sq_done")
        ss_done = sem("ss_done")
        root = sem("root")
        inv = sem("inv")
        unit = sem("unit")
        gc_row = sem("gc_row"); exp_row = sem("exp_row"); diff = sem("diff"); dec_exp = sem("dec_exp"); dec = sem("dec")
        qd_done = sem("qd_done")
        gram = sem("gram"); qk = sem("qk"); L_done = sem("L_done"); attn_done = sem("attn_done")
        LT_ps = sem("LT_ps"); attnT_ps = sem("attnT_ps"); v_ps = sem("v_ps"); k_ps = sem("k_ps")
        LT_done = sem("LT_done"); attnT_done = sem("attnT_done"); vb_done = sem("vb_done"); kd_done = sem("kd_done")
        x_init = sem("x_init")
        lx = sem("lx"); am = sem("am"); xat = sem("xat"); xtu = sem("xtu")
        xa = sem("xa"); xu = sem("xu")
        vn_ps = sem("vn_ps"); vn_done = sem("vn_done")
        ks = sem("ks"); rr_done = sem("rr_done"); s_ps = sem("s_ps"); s_done = sem("s_done")
        o_ps = sem("o_ps"); o_sq = sem("o_sq"); o_ss = sem("o_ss"); o_root = sem("o_root"); o_inv = sem("o_inv")
        o_nrm = sem("o_nrm"); o_done = sem("o_done")

        v_T = sem("v_T"); v_tok = sem("v_tok"); at_small = sem("at_small")
        sc_ps = sem("sc_ps"); sc_b = sem("sc_b"); mx = sem("mx"); nmx = sem("nmx"); pexp = sem("pexp")
        den = sem("den"); rec = sem("rec"); pn = sem("pn"); pt_ps = sem("pt_ps"); pt = sem("pt")
        at_ps = sem("at_ps"); at_out = sem("at_out")
        mix_hi = sem("mix_hi"); mix_lo = sem("mix_lo"); ld_h = sem("ld_h"); y_ps = sem("y_ps"); y_out = sem("y_out")
        ld_ln1 = sem("ld_ln1"); l1_stats = sem("l1_stats"); l1_step = sem("l1_step"); l1_root = sem("l1_root")
        l1_norm = sem("l1_norm"); l1_gain = sem("l1_gain"); h1_done = sem("h1_done"); h1_stored = sem("h1_stored")
        h1T_ps = sem("h1T_ps"); h1T_done = sem("h1T_done"); logits = sem("logits")
        rt = sem("rt"); rt_exp = sem("rt_exp"); rt_ps = sem("rt_ps"); table_zeroed = sem("table_zeroed"); table_zero = sem("table_zero")
        scattered = sem("scattered")
        gu_loaded = [sem(f"gu_loaded{i}") for i in range(4)]; dn_loaded = [sem(f"dn_loaded{i}") for i in range(4)]
        idx_loaded = sem("idx_loaded"); idx_read = sem("idx_read"); placed_ = sem("placed"); gathered = sem("gathered"); xT_ps = sem("xT_ps"); xT_a = sem("xT_a"); xT_d = sem("xT_d")
        gu_used = sem("gu_used"); sg_done = sem("sg_done"); hid_done = sem("hid_done"); hT_ps = sem("hT_ps")
        hidT_done = sem("hidT_done"); dn_used = sem("dn_used"); yw_done = sem("yw_done"); yw_hi = sem("yw_hi"); yw_split = sem("yw_split"); comb_ps = sem("comb_ps"); comb_done = sem("comb_done"); scaled = sem("scaled")
        ld_ln2 = sem("ld_ln2")
        f_step = sem("f_step"); f_root = sem("f_root"); f_norm = sem("f_norm"); f_gain = sem("f_gain"); f_done = sem("f_done"); f_done_p = sem("f_done_p")
        out_stored = sem("out_stored")

        Q0 = 1 + 4 * (HEADS + 1)
        O0 = STRIPS

        def W(eng, s, n):
            if not (isinstance(n, int) and n <= 0):
                eng.wait_ge(s, n)

        RT_GE, RT_D, RT_M = 3, 20, 23
        RT_DEST = RT_M + 7 + 2 + 4 + 2
        RT_ALL = RT_DEST + 3 + (CAP // SLOTS - 1) + 1 + 12
        def f_var(t):
            return 5 * (t + 1) + 2 * max(t - 1, 0)

        def f_bias(t):
            return f_var(min(t + 1, TT - 1)) + 2 * (1 + (t == TT - 1))

        BEFORE_HID = 12

        def piece(c, by_tile):
            return divmod(c, 4) if by_tile else divmod(c, TT)[::-1]

        def nth(n, per, k):
            return n * per + (k + 1 - per)

        def slot(j):
            return (1 + j) % 2

        def loads(it, j):
            return 16 * (2 * it + (1 + j) // 2 + 1)

        LN_VAR, LN_BIAS, LN_PER = 5, 7, 9
        BD_E, BD_G, BD_GC = 6, 15, 18

        block = ctx.enter_context(nc.Block())

        @block.sync
        def _(sp):
            sp.dma_start(xt[0][:, :], x2[:, 0, :]).then_inc(ld_x[0], 16)
            sp.dma_start(g0[:, :], ln0_g.partition_broadcast(P)).then_inc(ld_g0, 16)
            sp.dma_start(b0[:, :], ln0_b.partition_broadcast(P)).then_inc(ld_g0, 16)
            sp.dma_start(xt[1][:, :], x2[:, 1, :]).then_inc(ld_x[1], 16)
            sp.dma_start(cst[:, :], consts).then_inc(ld_const, 16)
            sp.dma_start(raw[0][:, :].rearrange("p (k n) -> p k n", k=KD),
                         w_in_v[:, :, C_BETA:C_BETA + P]).then_inc(raw_loaded[0], 16)
            for t in range(2, TT):
                sp.wait_ge(ln_norm, t - 1)
                sp.dma_start(xt[t % 2][:, :], x2[:, t, :]).then_inc(ld_x[t % 2], 16)
                if t == 2:
                    sp.dma_start(rc[:, :], route_consts[:, 0:3 * E + TT]).then_inc(ld_small, 16)
                    sp.dma_start(cwraw[:, :], conv_w[0].rearrange("a (c p) -> (a c) p", p=P)).then_inc(ld_small, 16)
                    sp.dma_start(ab[:, 0, :], a_log[0].partition_broadcast(P)).then_inc(ld_small, 16)
                    sp.dma_start(ab[:, 1, :], dt_bias[0].partition_broadcast(P)).then_inc(ld_small, 16)
                    sp.dma_start(nrm[:, :], gdn_norm_w[0].rearrange("(p o) -> p o", o=1)).then_inc(ld_small, 16)
                    sp.dma_start(attn_small[:, QH:], sinks[0].partition_broadcast(P)).then_inc(ld_small, 16)
                    sp.dma_start(attn_small[:, 0:QH], att_consts[:, J_SLOPE:J_END]).then_inc(ld_small, 16)

            def strip_loads(it, cols, js=range(4)):
                for j in js:
                    W(sp, strip_lo, 4 * it + j)
                    sp.dma_start(raw[slot(j)][:, :].rearrange("p (k n) -> p k n", k=KD),
                                 cols(j)).then_inc(raw_loaded[slot(j)], 16)

            def head_cols(it):
                return lambda j: w_in_v[:, :, bass.ds(it * P + j * HEADS * DK, P)]

            strip_loads(0, head_cols(0), js=[0])
            strip_loads(0, head_cols(0), js=[1, 2, 3])
            with sp.Fori(1, HEADS) as it:
                strip_loads(it, head_cols(it))
            strip_loads(HEADS, lambda j: w_in_v[:, :, C_BK + P * j:C_BK + P * (j + 1)])
            sp.wait_ge(silu[2], HEADS)
            sp.wait_ge(silu[3], HEADS)
            sp.dma_start(dist[:, :, :], att_consts[:, 0:6 * P].rearrange("p (a b) -> p a b", a=3)).then_inc(ld_att, 16)

            def ring_load(s_, sl_, src, k):
                W(sp, strip_lo, s_ - 1)
                sp.dma_start(raw[sl_][:, :].rearrange("p (k n) -> p k n", k=k), src).then_inc(raw_loaded[sl_], 16)

            with sp.Fori(0, 4) as m:
                for j in range(2):
                    ring_load(2 * m + (Q0 + j), slot(j), w_in_v[:, :, bass.ds(m * (2 * P) + (C_BQ + P * j), P)], KD)
            def o_loads(nt):
                for kg_ in range(4):
                    ring_load(4 * nt + (O0 + kg_), slot(kg_),
                              w_o_v[:, 4 * kg_:4 * kg_ + 4, bass.ds(nt * S, S)], 4)

            o_loads(0)
            sp.wait_ge(mix_lo, 4)
            for i in range(2):
                sp.wait_ge(h_stored[i], 16 * TT // 2)
            sp.dma_start(r1[:, :, :], h_scr_v).then_inc(ld_h, 16)
            sp.dma_start(g1[:, :], ln1_g[0].partition_broadcast(P)).then_inc(ld_ln1, 16)
            sp.dma_start(b1[:, :], ln1_b[0].partition_broadcast(P)).then_inc(ld_ln1, 16)
            sp.dma_start(tokens[:, :], route_consts[:, 3 * E + TT:]).then_inc(ld_ln1, 16)
            sp.dma_start(wr[:, :, 0:GROUPS], w_route_group[0].rearrange("(k p) n -> p k n", p=P)).then_inc(ld_ln1, 16)
            sp.dma_start(wr[:, :, GROUPS:], w_route_expert[0].rearrange("(k p) n -> p k n", p=P)).then_inc(ld_ln1, 16)
            with sp.Fori(1, 4) as nt:
                o_loads(nt)
            sp.wait_ge(strip_mm, STRIPS + PIECES)
            sp.dma_start(g2[:, :], ln2_g[0].partition_broadcast(P)).then_inc(ld_ln2, 16)
            sp.dma_start(b2[:, :], ln2_b[0].partition_broadcast(P)).then_inc(ld_ln2, 16)

            def expert_weights(t, e):
                for i in range(12):
                    if i < 8:
                        W(sp, gu_used, 4 * t + (i // 2 - 3))
                        src = [gate_v, up_v][i % 2][:, bass.ds(e, 1), 4 * (i // 2):4 * (i // 2) + 4, :]
                        sp.dma_start(wpiece[i][:, :].rearrange("p (k f) -> p k f", k=4),
                                     src.rearrange("p o k f -> p (o k) f")).then_inc(gu_loaded[i // 2], 16)
                    else:
                        W(sp, dn_used, 4 * t + (i - 8 - 3))
                        src = down_v[:, bass.ds(e, 1), i - 8:i - 7, :]
                        sp.dma_start(wpiece[i][:, :], src.rearrange("p o c n -> p (o c n)")).then_inc(dn_loaded[i - 8], 16)

            expert_weights(0, 0)
            with sp.Fori(1, E) as t:
                expert_weights(t, t)
            sp.wait_ge(rt, RT_ALL)
            left = sp.value_load(ovi[0:1, 2 * LEFTOVER:2 * LEFTOVER + 1], min_val=0, max_val=LEFTOVER)
            with sp.If(left > 0):
                with sp.Fori(0, left) as i:
                    e = sp.value_load(ovi[0:1, bass.ds(i, 1)], min_val=0, max_val=E - 1)
                    expert_weights(i + E, e)
            for t in range(TT):
                sp.wait_ge(f_done_p if t < TT - 1 else f_done, t + 1 if t < TT - 1 else 1)
                sp.dma_start(out2[:, t, :], r1[:, t, :]).then_inc(out_stored, 16)
            sp.wait_ge(out_stored, 16 * TT)

        @block.gpsimd
        def _(pool):
            pool.memset(unused[:, :], 0).then_inc(table_zeroed, 1)
            pool.wait_ge(table_zeroed, 1)
            pool.dma_start(slot_rows.rearrange("(p n) o -> p (n o)", p=P), unused[:, :]).then_inc(table_zero, 16)
            pool.memset(eps[:, 0:1], LN_EPS).then_inc(zero_pad, 1)
            pool.memset(eps[:, 1:2], RMS_EPS).then_inc(zero_pad, 1)
            pool.wait_ge(ln_step, LN_PER * TT)
            pool.wait_ge(hT_psum, 2 * TT * 2)
            for j in range(3):
                pool.memset(xp[j][:, 0:CONV - 1], 0.0).then_inc(zero_pad, 1)

            def lo(s, sl):
                pool.wait_ge(strip_hi, s + 1)
                W(pool, strip_mm, s - 1)
                pool.tensor_tensor(wlo[sl][:, :, :].rearrange("p k n -> p (k n)"), raw[sl][:, :],
                                   whi[sl][:, :, :].rearrange("p k n -> p (k n)").bitcast(F32),
                                   ALU.subtract).then_inc(strip_lo, 1)

            lo(0, 0)
            lo(1, 1)

            def iteration(it, gdn=True, last=False):
                for j in range(4):
                    lo(4 * it + 2 + j, slot(j + 1))
                    if j == 0 and gdn:
                        pool.wait_ge(par_done, 1)
                        pool.wait_ge(dec_exp, it)
                        ed = T["Ed"][:, :].rearrange("p (c i) -> p c i", c=TT)
                        pool.affine_select(out=ed, in_=ed, compare_op=ALU.is_ge, fill=0.0, base=0,
                                           pattern=[[0, TT], [-1, P]], channel_multiplier=1).then_inc(dec, 1)
                        if last:
                            for i in range(3):
                                pool.wait_ge(silu[i], HEADS)
                            pool.memset(kdup[:, :, 0:P], 0.0).then_inc(kpad, 1)

            iteration(0, gdn=False)
            with pool.Fori(1, HEADS) as it:
                iteration(it)
            iteration(HEADS, last=True)
            with pool.Fori(0, 4) as m:
                for j in range(2):
                    lo(2 * m + (Q0 + 1 + j), j)
            with pool.Fori(0, 3) as nt:
                for kg_ in range(4):
                    lo(4 * nt + (O0 + 1 + kg_), kg_ % 2)
            for kg_ in range(3):
                lo(O0 + 13 + kg_, kg_ % 2)
            pool.wait_ge(table_zero, 16)
            pool.wait_ge(rt, RT_DEST)
            for t in range(TT):
                for c in range(2):
                    pool.indirect_dma_start(slot_rows, bass.IndirectOffsetOnAxis(ap=rd[:, t, c:c + 1], axis=0),
                                            toki[:, t, c, :], None).then_inc(scattered, 16)
            pool.wait_ge(scattered, 16 * 2 * TT)
            pool.wait_ge(rt, RT_ALL)
            pool.wait_ge(logits, 1)
            pool.wait_ge(h1_stored, 16 * TT)
            r_idx, r_free = pool.alloc_register("r_idx"), pool.alloc_register("r_free")

            def gather(t, row):
                W(pool, gathered, 16 * t)
                W(pool, idx_read, t)
                for h in range(2):
                    pool.dma_start(idx[SLOTS * h:SLOTS * (h + 1), :], slot_rows[bass.ds(row, SLOTS), :]).then_inc(idx_loaded, 16)
                pool.reg_mov(r_idx, 32 * t + 32)
                pool.reg_mov(r_free, 2 * t)
                pool.wait_ge(h1_stored, 16 * TT)
                pool.wait_ge(idx_loaded, r_idx)
                if not isinstance(t, int):
                    pool.wait_ge(xT_ps, r_free)
                pool.indirect_dma_start(xb[:, :], None, h1_scr,
                                        bass.IndirectOffsetOnAxis(ap=idx[0:SLOTS, 0:1], axis=0)).then_inc(gathered, 16)

            gather(0, 0)
            with pool.Fori(1, E) as t:
                gather(t, t * CAP)
            left = pool.value_load(ovi[0:1, 2 * LEFTOVER:2 * LEFTOVER + 1], min_val=0, max_val=LEFTOVER)
            with pool.If(left > 0):
                with pool.Fori(0, left) as i:
                    row = pool.value_load(ovi[0:1, bass.ds(i + LEFTOVER, 1)], min_val=0, max_val=E * CAP - SLOTS)
                    gather(i + E, row)
            for t in range(TT - 1):
                pool.wait_ge(f_gain, t + 1)
                pool.wait_ge(ld_ln2, 32)
                pool.tensor_tensor(r1[:, t, :], r1[:, t, :], b2[:, :], ALU.add).then_inc(f_done_p, 1)

        @block.scalar
        def _(act):
            def copy(o_, i_, s, scale=1.0):
                return act.activation(o_, i_, ACT.Copy, scale=scale).then_inc(s, 1)

            act.wait_ge(zero_pad, 2)
            for t in range(TT):
                act.wait_ge(ln_step, LN_PER * t + LN_VAR)
                act.activation(rstd[:, :], mv[:, 1:2], ACT.Sqrt, bias=eps[:, 0:1]).then_inc(ln_sqrt, 1)
                act.wait_ge(ln_step, LN_PER * t + LN_BIAS)
                W(act, hT_psum, 4 * (t - 1))
                if t >= 2:
                    act.wait_ge(h_stored[t % 2], 16 * (t // 2))
                act.activation(xn[t % 2][:, :], xt[t % 2][:, :], ACT.Identity, bias=nmr[:, 0:1],
                               scale=rstd[:, 0:1]).then_inc(ln_norm, 1)
                act.wait_ge(ln_step, LN_PER * (t + 1))
                act.dma_start(h_scr_v[:, t, :], xn[t % 2][:, :]).then_inc(h_stored[t % 2], 16)
                for b in range(4):
                    act.wait_ge(hT_psum, 4 * t + b + 1)
                    act.activation(hTh[:, 4 * b:4 * b + 4, t * P:(t + 1) * P],
                                   banks[4 + b][:, :].rearrange("p (k n) -> p k n", k=4),
                                   ACT.Copy).then_inc(hT_hi, 1)

            def hi(s, sl, landed):
                act.wait_ge(raw_loaded[sl], landed)
                W(act, strip_mm, s - 1)
                act.activation(whi[sl][:, :, :].rearrange("p k n -> p (k n)"), raw[sl][:, :],
                               ACT.Copy).then_inc(strip_hi, 1)

            hi(0, 0, 16)
            hi(1, 1, 16)
            for i in range(2):
                act.wait_ge(h_stored[i], 16 * TT // 2)
            act.wait_ge(strip_mm, 1)
            act.activation(bd[:, :], PA[0][:, :], ACT.Copy).then_inc(strip_out, 1)
            act.wait_ge(bd_done, 3)
            act.activation(wk[:, 0, :, :], wk[:, 0, :, :], ACT.Exp, scale=-1.0).then_inc(bda, 1)
            act.activation(ab[:, 0, :], ab[:, 0, :], ACT.Exp).then_inc(bda, 1)
            act.activation(wk[:, 2, :, :], wk[:, 1, :, :], ACT.Abs).then_inc(bda, 1)
            act.wait_ge(bda, 3)
            act.activation(wk[:, 2, :, :], wk[:, 2, :, :], ACT.Exp, scale=-1.0).then_inc(bda, 1)
            act.wait_ge(bd_done, BD_E)
            act.activation(wk[:, 4, :, :], wk[:, 3, :, :], ACT.Ln).then_inc(bda, 1)
            act.wait_ge(bd_done, BD_GC)
            act.activation(wk[:, 3, :, :], wk[:, 2, :, :], ACT.Exp).then_inc(bda, 1)
            act.activation(wk[:, 4, :, :], wk[:, 4, :, :], ACT.Exp).then_inc(bda, 1)
            act.activation(wk[:, 5, :, :], wk[:, 5, :, :], ACT.Exp).then_inc(bda, 1)

            def out_qkv(it, j):
                act.wait_ge(strip_mm, 4 * it + 2 + j)
                W(act, taps, 3 * CONV * it + CONV * (j - 2) if not isinstance(it, int) or it else 0)
                act.activation(xp[j][:, CONV - 1:CONV - 1 + S], PA[slot(j)][:, :], ACT.Copy).then_inc(strip_out, 1)

            def out_z(it):
                act.wait_ge(strip_mm, 4 * it + 5)
                act.activation(half[3][:, :], PA[0][:, :], ACT.Copy, scale=0.5)
                act.activation(th[3][:, :], PA[0][:, :], ACT.Tanh, scale=0.5).then_inc(strip_out, 1)

            def tanh(it, j):
                act.wait_ge(taps, 3 * CONV * it + CONV * (j + 1))
                W(act, silu[j], it)
                act.activation(th[j][:, :], half[j][:, :], ACT.Tanh).then_inc(tanh_done, 1)

            def gdn0(n):
                for j in range(2):
                    act.wait_ge(silu[j], n)
                    act.activation(T[["dm", "L"][j]][:, :], T[["q", "k"][j]][:, :], ACT.Square).then_inc(sq_done, 1)
                for j in range(2):
                    act.wait_ge(ss_done, nth(n, 2, j))
                    act.activation(T[["X", "XT"][j]][:, :], [B0, B1][j][:, :], ACT.Sqrt, bias=eps[:, 1:2]).then_inc(root, 1)
                act.wait_ge(gc_row, n)
                act.activation(T["qd"][:, :], B2[:, :], ACT.Exp).then_inc(exp_row, 1)
                act.wait_ge(diff, 4 * n)
                act.activation(T["Ed"][:, :], T["dm"][:, :], ACT.Exp, scale=-1.0).then_inc(dec_exp, 1)

            def gdn1(n):
                act.wait_ge(LT_ps, n)
                act.activation(T["LT"][:, :], B2[:, :], ACT.Copy).then_inc(LT_done, 1)
                act.wait_ge(attnT_ps, n)
                act.activation(T["attnT"][:, :], BM[:, :], ACT.Copy).then_inc(attnT_done, 1)

            def gdn3(n):
                for c in range(TT):
                    act.wait_ge(vn_ps, nth(n, TT, c))
                    act.activation(vn[:, :], BS[:, P:2 * P], ACT.Copy).then_inc(vn_done, 1)
                act.wait_ge(o_ps, n)
                act.activation(T["A"][:, :], BO[:, :], ACT.Square).then_inc(o_sq, 1)
                act.wait_ge(o_ss, n)
                act.activation(T["L"][:, :], BM[:, :], ACT.Sqrt, bias=eps[:, 1:2], scale=1.0 / DK).then_inc(o_root, 1)

            def next_hi(it, j):
                hi(4 * it + 2 + j, slot(j + 1), loads(it, j + 1))

            def iteration(it, gdn=True, last=False):
                next_hi(it, 0)
                if gdn:
                    out_z(it - 1)
                    gdn0(it)
                next_hi(it, 1)
                out_k(0) if last else out_qkv(it, 0)
                if gdn:
                    gdn1(it)
                if not last:
                    tanh(it, 0)
                next_hi(it, 2)
                out_k(1) if last else out_qkv(it, 1)
                if not last:
                    tanh(it, 1)
                next_hi(it, 3)
                out_v(0) if last else out_qkv(it, 2)
                if gdn:
                    gdn3(it)
                if not last:
                    tanh(it, 2)

            def out_k(j):
                act.wait_ge(strip_mm, 4 * HEADS + 2 + j)
                if j == 0:
                    for i in range(3):
                        act.wait_ge(silu[i], HEADS)
                    act.wait_ge(kpad, 1)
                for g in range(2):
                    for r in range(2):
                        i = act.activation(kdup[HD * r:HD * (r + 1), 2 * j + g, P:P + S],
                                           PA[slot(j)][HD * g:HD * (g + 1), :], ACT.Copy)
                i.then_inc(strip_out, 1)

            def out_v(j):
                act.wait_ge(strip_mm, 4 * HEADS + 4 + j)
                act.wait_ge(silu[3], HEADS)
                act.activation(vT[:, j, :], PA[slot(j + 2)][:, :], ACT.Copy).then_inc(strip_out, 1)

            iteration(0, gdn=False)
            with act.Fori(1, HEADS) as it:
                iteration(it)
            iteration(HEADS, last=True)

            def attend(m, j):
                u = 2 * m + j
                for r in range(2):
                    act.wait_ge(nmx, 2 * u + (r + 1))
                    act.activation(att8[:, 3, 4 * r:4 * r + 4], att8[:, 1, 4 * r:4 * r + 4], ACT.Exp,
                                   bias=sl[:, 1, 2 * j + r:2 * j + r + 1])
                    for t in range(TT):
                        v = sc[:, r, t // 2, t % 2, :]
                        i = act.activation(v, v, ACT.Exp, bias=att8[:, 1, 4 * r + t:4 * r + t + 1],
                                           accum_out=att8[:, 2, 4 * r + t:4 * r + t + 1])
                i.then_inc(pexp, 1)
                for i in range(4):
                    act.wait_ge(pt_ps, 4 * u + (i + 1))
                    act.activation(pT[:, i, :], [BS, BO, B0, B1][i][:, :], ACT.Copy).then_inc(pt, 1)
                act.wait_ge(at_ps, u + 1)
                act.activation(mixT[:, bass.ds(u + HEADS, 1), :].rearrange("p o s -> p (o s)"), B2[:, :],
                               ACT.Copy).then_inc(at_out, 1)

            def out_q(u, j):
                act.wait_ge(strip_mm, u + (Q0 + 1))
                act.activation(aq[j][:, :], PA[slot(j)][:, :], ACT.Copy, scale=float(HD) ** -0.5).then_inc(strip_out, 1)

            def q_hi(m, j):
                hi(2 * m + (Q0 + 1 + j), j, 16 * m + 16 * ((Q0 + 1) // 2 + 1))

            q_hi(0, 0)
            out_v(1)
            for j in range(2):
                act.wait_ge(v_T, j + 1)
                act.activation(vtok[:, :, P * j:P * (j + 1)],
                               [B0, B1][j][:, :].rearrange("p (t n) -> p t n", t=TT), ACT.Copy).then_inc(v_tok, 1)
            act.wait_ge(o_done, HEADS)
            q_hi(0, 1)
            out_q(0, 0)
            with act.Fori(1, 4) as m:
                q_hi(m, 0)
                out_q(2 * m - 1, 1)
                attend(m - 1, 0)
                q_hi(m, 1)
                out_q(2 * m, 0)
                attend(m - 1, 1)
            q_hi(4, 0)
            out_q(7, 1)

            def split_mix(i):
                act.activation(mxh[:, 4 * i:4 * i + 4, :], mixT[:, 4 * i:4 * i + 4, :], ACT.Copy).then_inc(mix_hi, 1)

            act.wait_ge(strip_mm, STRIPS)
            act.wait_ge(at_out, 4)
            for i in range(3):
                split_mix(i)
            attend(3, 0)
            attend(3, 1)
            act.wait_ge(at_out, 8)
            split_mix(3)

            def o_hi(nt, kg_):
                hi(4 * nt + (O0 + 1 + kg_), kg_ % 2, 32 * nt + 16 * ((O0 + 1 + kg_) // 2 + 1))

            for kg_ in range(1, 4):
                o_hi(0, kg_)
            with act.Fori(1, 3) as nt:
                for kg_ in range(4):
                    o_hi(nt, kg_)
            for kg_ in range(3):
                o_hi(3, kg_)

            act.wait_ge(l1_step, 4)
            act.activation(rs4[:, :], mv4[:, :, 1:2].rearrange("p t o -> p (t o)"), ACT.Sqrt, bias=eps[:, 0:1]).then_inc(l1_root, 1)
            act.wait_ge(l1_step, 6)
            for t in range(TT):
                act.activation(r1[:, t, :], r1[:, t, :], ACT.Identity, bias=nm4[:, t:t + 1], scale=rs4[:, t:t + 1]).then_inc(l1_norm, 1)
            for t in range(TT):
                act.wait_ge(h1_done, t + 1)
                act.dma_start(h1_scr_v[:, t, :], r1[:, t, :]).then_inc(h1_stored, 16)
                for b in range(4):
                    act.wait_ge(h1T_ps, 4 * t + b + 1)
                    act.activation(h1T[:, 4 * b:4 * b + 4, t * P:(t + 1) * P],
                                   [PA[0], PA[1], BS, BO][b][:, :].rearrange("p (k n) -> p k n", k=4), ACT.Copy).then_inc(h1T_done, 1)
            act.wait_ge(rt, RT_GE)
            act.activation(ge[:, :, :], ge[:, :, :], ACT.Exp).then_inc(rt_exp, 1)
            act.wait_ge(rt, RT_D)
            act.activation(wts[:, 1, :], wts[:, 0, :], ACT.Exp).then_inc(rt_exp, 1)

            def block_act(t):
                act.wait_ge(xT_ps, 2 * t + 1)
                W(act, gu_used, 4 * t)
                act.activation(xbT[:, 0:8, :], PA[0][:, :].rearrange("p (k n) -> p k n", k=8), ACT.Copy).then_inc(xT_a, 1)
                act.wait_ge(gu_used, 4 * t + 4)
                W(act, hT_ps, t)
                act.activation(hid[SLOTS:P, :], B0[0:SLOTS, :], ACT.Silu).then_inc(sg_done, 1)
                act.wait_ge(hT_ps, t + 1)
                W(act, dn_used, 4 * t)
                act.activation(hidT[:, :, :], B1[:, 0:KF * SLOTS].rearrange("p (c n) -> p c n", c=KF), ACT.Copy).then_inc(hidT_done, 1)
                act.wait_ge(dn_used, 4 * t + 4)
                act.wait_ge(idx_read, t + 1)
                W(act, yw_split, 4 * t)
                for q in range(4):
                    j, h = divmod(q, 2)
                    for o_ in range(2):
                        half_ = slice(SLOTS * o_, SLOTS * (o_ + 1))
                        i = act.activation(yw[half_, q, :], [B2, BM][j][SLOTS * h:SLOTS * (h + 1), :], ACT.Copy,
                                           scale=slot_tw[half_, 1:2])
                    i.then_inc(yw_done, 1)

            act.wait_ge(h1_stored, 16 * TT)
            act.wait_ge(h1T_ps, 4 * TT)
            for t in range(TT):
                act.activation(r1[:, t, :], r1[:, t, :], ACT.Copy, scale=ALPHA).then_inc(scaled, 1)
            act.wait_ge(rt, RT_ALL)
            block_act(0)
            with act.Fori(1, E) as t:
                block_act(t)
            left = act.value_load(ovi[0:1, 2 * LEFTOVER:2 * LEFTOVER + 1], min_val=0, max_val=LEFTOVER)
            with act.If(left > 0):
                with act.Fori(0, left) as i:
                    block_act(i + E)
            for t in range(TT):
                act.wait_ge(f_step, f_var(t))
                act.activation(rs4[:, t:t + 1], mv4[:, t, 1:2], ACT.Sqrt, bias=eps[:, 0:1]).then_inc(f_root, 1)
                act.wait_ge(f_step, f_bias(t))
                act.activation(r1[:, t, :], r1[:, t, :], ACT.Identity, bias=nm4[:, t:t + 1], scale=rs4[:, t:t + 1]).then_inc(f_norm, 1)

        @block.vector
        def _(dve):
            dve.wait_ge(ld_g0, 32)
            for t in range(TT):
                dve.wait_ge(ld_x[t % 2], 16 * (t // 2 + 1))
                W(dve, ln_sqrt, t)
                for q in range(4):
                    i = dve.bn_stats(bns[:, q, :], xt[t % 2][:, q * 512:(q + 1) * 512])
                    i.then_inc(ln_step, 1)
                dve.wait_ge(ln_step, LN_PER * t + 4)
                dve.bn_aggr(mv[:, :], bns[:, :, :].rearrange("p a b -> p (a b)")).then_inc(ln_step, 1)
                dve.wait_ge(ln_sqrt, t + 1)
                W(dve, ln_norm, t)
                dve.reciprocal(rstd[:, :], rstd[:, :]).then_inc(ln_step, 1)
                dve.wait_ge(ln_step, LN_PER * t + LN_VAR + 1)
                dve.scalar_tensor_tensor(out=nmr[:, :], in0=mv[:, 0:1], scalar=-1.0, in1=rstd[:, :],
                                         op0=ALU.mult, op1=ALU.mult).then_inc(ln_step, 1)
                dve.wait_ge(ln_norm, t + 1)
                dve.tensor_tensor(xn[t % 2][:, :], xn[t % 2][:, :], g0[:, :], ALU.mult).then_inc(ln_step, 1)
                dve.wait_ge(ln_step, LN_PER * t + LN_BIAS + 1)
                dve.tensor_tensor(xn[t % 2][:, :], xn[t % 2][:, :], b0[:, :], ALU.add).then_inc(ln_step, 1)
                for b in range(4):
                    dve.wait_ge(hT_hi, 4 * t + b + 1)
                    o_ = hTl[:, 4 * b:4 * b + 4, t * P:(t + 1) * P]
                    dve.tensor_tensor(o_, banks[4 + b][:, :].rearrange("p (k n) -> p k n", k=4),
                                      hTh[:, 4 * b:4 * b + 4, t * P:(t + 1) * P].bitcast(F32),
                                      ALU.subtract).then_inc(hT_lo, 1)
            dve.wait_ge(cw_psum, 1)
            dve.tensor_copy(cw[:, :], BM[:, 0:CONV * 24]).then_inc(cw_done, 1)
            dve.wait_ge(bd_T, 1)
            pv = B0[:, 0:TT * 2 * HEADS].rearrange("p (c n) -> p c n", c=TT)
            dve.tensor_copy(bdt[:, :, :], pv).then_inc(bd_done, 1)
            dve.wait_ge(bd_done, 1)
            dve.wait_ge(ld_small, 16 * 7)
            dve.tensor_copy(wk[:, 0, :, :], bdt[:, :, 0:HEADS]).then_inc(bd_done, 1)
            dve.tensor_tensor(wk[:, 1, :, :], bdt[:, :, HEADS:], ab[:, 1:2, :].broadcast_to([P, TT, HEADS]),
                              ALU.add).then_inc(bd_done, 1)
            dve.wait_ge(bda, 4)
            n = [3]

            def link(i):
                n[0] += 1
                i.then_inc(bd_done, 1)
                dve.wait_ge(bd_done, n[0])

            w_ = lambda i: wk[:, i, :, :]
            link(dve.tensor_scalar(w_(0), w_(0), 1.0, None, ALU.add))
            link(dve.reciprocal(w_(0), w_(0)))
            link(dve.tensor_scalar(w_(3), w_(2), 1.0, None, ALU.add))
            link(dve.tensor_scalar(w_(5), w_(3), 1.0, None, ALU.is_equal))
            link(dve.tensor_tensor(w_(5), w_(5), w_(2), ALU.mult))
            dve.wait_ge(bda, 5)
            link(dve.tensor_scalar(w_(3), w_(3), 1.0, 1e-30, ALU.subtract, ALU.max))
            link(dve.reciprocal(w_(3), w_(3)))
            link(dve.tensor_tensor(w_(3), w_(3), w_(2), ALU.mult))
            link(dve.tensor_tensor(w_(3), w_(3), w_(4), ALU.mult))
            link(dve.tensor_tensor(w_(3), w_(3), w_(5), ALU.add))
            link(dve.scalar_tensor_tensor(out=w_(3), in0=w_(1), scalar=0.0, in1=w_(3), op0=ALU.max, op1=ALU.add))
            link(dve.scalar_tensor_tensor(out=w_(1), in0=w_(3), scalar=-1.0,
                                          in1=ab[:, 0:1, :].broadcast_to([P, TT, HEADS]), op0=ALU.mult, op1=ALU.mult))
            assert n[0] == BD_G
            dve.wait_ge(gcum, 1)
            gcv = B0[:, 128:128 + TT * HEADS].rearrange("p (c n) -> p c n", c=TT)
            glv = B0[:, 256:256 + TT * HEADS].rearrange("p (c n) -> p c n", c=TT)
            link(dve.tensor_copy(w_(2), gcv))
            link(dve.tensor_copy(w_(5), glv))
            link(dve.tensor_tensor(w_(4), w_(5), w_(2), ALU.subtract))
            tp = lambda i: tokpar[:, :, i, :].rearrange("p h c -> p c h")
            link(dve.tensor_copy(tp(0), w_(1)))
            link(dve.tensor_copy(tp(1), w_(0)))
            link(dve.tensor_copy(tp(2), w_(2)))
            dve.wait_ge(bda, 8)
            link(dve.scalar_tensor_tensor(out=tp(3), in0=w_(0), scalar=-1.0, in1=w_(3), op0=ALU.mult, op1=ALU.mult))
            link(dve.tensor_copy(tp(4), w_(4)))
            dve.tensor_copy(tp(5), w_(5)).then_inc(par_done, 1)

            def conv(it, j):
                dve.wait_ge(strip_out, 4 * it + 2 + j)
                dve.wait_ge(conv_w_ready, it + 1)
                W(dve, silu[j], it)
                dve.tensor_scalar(half[j][:, :], xp[j][:, 0:S], cwh[:, 0, j:j + 1], None, ALU.mult).then_inc(taps, 1)
                for a in range(1, CONV):
                    dve.wait_ge(taps, 3 * CONV * it + (CONV * j + a))
                    dve.scalar_tensor_tensor(out=half[j][:, :], in0=xp[j][:, a:a + S], scalar=cwh[:, a, j:j + 1],
                                             in1=half[j][:, :], op0=ALU.mult, op1=ALU.add).then_inc(taps, 1)

            def conv_weights(it):
                W(dve, taps, 3 * CONV * it)
                view = cw[:, :].rearrange("p (a j h) -> p h a j", a=CONV, j=3)
                dve.tensor_scalar(cwh[:, :, :], view[:, bass.ds(it, 1), :, :].rearrange("p o a j -> p (o a) j"), 0.5,
                                  None, ALU.mult).then_inc(conv_w_ready, 1)

            def act_silu(j, n):
                if j < 3:
                    dve.wait_ge(tanh_done, nth(n, 3, j))
                else:
                    dve.wait_ge(strip_out, 4 * n + 1)
                dve.scalar_tensor_tensor(out=T[["q", "k", "v", "sz"][j]][:, :], in0=th[j][:, :], scalar=1.0,
                                         in1=half[j][:, :], op0=ALU.add, op1=ALU.mult).then_inc(silu[j], 1)

            def tiles(name):
                return T[name][:, :].rearrange("p (c i) -> p c i", c=TT)

            def psum_tiles(b):
                return b[:, :].rearrange("p (c i) -> p c i", c=TT)

            def over(col):
                return hp[:, col, :].rearrange("p (c o) -> p c o", o=1).broadcast_to([P, TT, P])

            def mask(l):
                return cst[:, K_MASK + l * P:K_MASK + (l + 1) * P].rearrange("p (o i) -> p o i", o=1).broadcast_to([P, TT, P])

            def wide(c0):
                return cst[:, c0:c0 + P].rearrange("p (o i) -> p o i", o=1).broadcast_to([P, TT, P])

            def gdn0(n):
                h = n - 1
                act_silu(0, n)
                act_silu(1, n)
                act_silu(2, n)
                dve.tensor_copy(hp[:, :, :].rearrange("p f c -> p (f c)"),
                                tokpar[:, bass.ds(h, 1), :, :].rearrange("p o f c -> p (o f c)")).then_inc(hp_ready, 1)
                dve.wait_ge(hp_ready, n)
                dve.tensor_copy(gb[:, :, :], over(0)).then_inc(gb_ready, 1)
                act_silu(3, n)
                for j in range(2):
                    dve.wait_ge(root, nth(n, 2, j))
                    t_ = T[["X", "XT"][j]]
                    dve.reciprocal(t_[:, :], t_[:, :]).then_inc(inv, 1)
                dve.wait_ge(exp_row, n)
                dve.wait_ge(ss_done, nth(n, 2, 0))
                for c in range(TT):
                    dve.tensor_scalar(tiles("dm")[:, c, :], B2[:, c * P:(c + 1) * P], hp[:, 2, c:c + 1], 0.0,
                                      ALU.subtract, ALU.max).then_inc(diff, 1)
                dve.wait_ge(inv, nth(n, 2, 0))
                dve.scalar_tensor_tensor(out=T["q"][:, :], in0=T["q"][:, :], scalar=float(DK) ** -0.5, in1=T["X"][:, :],
                                         op0=ALU.mult, op1=ALU.mult).then_inc(unit, 1)
                dve.wait_ge(inv, nth(n, 2, 1))
                dve.tensor_tensor(T["k"][:, :], T["k"][:, :], T["XT"][:, :], ALU.mult).then_inc(unit, 1)
                dve.wait_ge(exp_row, n)
                dve.wait_ge(unit, nth(n, 2, 0))
                dve.tensor_tensor(T["qd"][:, :], T["qd"][:, :], T["q"][:, :], ALU.mult).then_inc(qd_done, 1)

            def gdn1(n):
                dve.wait_ge(dec, n)
                dve.wait_ge(gram, n)
                for c in range(TT):
                    i = dve.scalar_tensor_tensor(out=tiles("L")[:, c, :], in0=B0[:, c * P:(c + 1) * P],
                                                 scalar=hp[:, 1, c:c + 1], in1=tiles("Ed")[:, c, :],
                                                 op0=ALU.mult, op1=ALU.mult)
                i.then_inc(L_done, 1)
                dve.wait_ge(qk, n)
                dve.wait_ge(gc_row, n)
                dve.tensor_tensor(T["A"][:, :], B1[:, :], T["Ed"][:, :], ALU.mult).then_inc(attn_done, 1)
                dve.wait_ge(L_done, n)
                dve.wait_ge(unit, 2 * n)
                dve.tensor_tensor(tiles("X"), tiles("L"), mask(0), ALU.mult).then_inc(x_init, 1)
                dve.wait_ge(x_init, nth(n, 4, 0))
                dve.tensor_tensor(tiles("X"), wide(K_ID), tiles("X"), ALU.subtract).then_inc(x_init, 1)
                dve.wait_ge(LT_done, n)
                dve.tensor_tensor(tiles("XT"), tiles("LT"), wide(K_M1T), ALU.mult).then_inc(x_init, 1)
                dve.wait_ge(x_init, nth(n, 4, 2))
                dve.tensor_tensor(tiles("XT"), wide(K_ID), tiles("XT"), ALU.subtract).then_inc(x_init, 1)
                dve.wait_ge(v_ps, n)
                dve.tensor_tensor(tiles("vb"), psum_tiles(B0), over(1), ALU.mult).then_inc(vb_done, 1)
                dve.wait_ge(k_ps, n)
                dve.tensor_tensor(tiles("kd"), psum_tiles(B1), over(4), ALU.mult).then_inc(kd_done, 1)

            def level(l, n):
                dve.wait_ge(lx, nth(n, LEVELS, l))
                if l == 0:
                    dve.wait_ge(attnT_ps, n)
                dve.tensor_tensor(tiles("A"), psum_tiles(B0), mask(l + 1), ALU.mult).then_inc(am, 1)
                if l < LEVELS - 1:
                    dve.wait_ge(xa, nth(n, LEVELS - 1, l))
                    if l:
                        dve.wait_ge(xu, nth(n, LEVELS - 1, l - 1))
                    dve.tensor_tensor(T["X"][:, :], T["X"][:, :], B1[:, :], ALU.subtract).then_inc(xu, 1)
                dve.wait_ge(xat, nth(n, LEVELS, l))
                dve.tensor_tensor(T["XT"][:, :], T["XT"][:, :], B2[:, :], ALU.subtract).then_inc(xtu, 1)

            def scan(n):
                for c in range(TT):
                    if c > 0:
                        dve.wait_ge(ks, nth(n, TT - 1, c - 1))
                        dve.scalar_tensor_tensor(out=rr[:, :], in0=BS[:, 0:P], scalar=hp[:, 3, c:c + 1],
                                                 in1=tiles("vb")[:, c, :], op0=ALU.mult, op1=ALU.add).then_inc(rr_done, 1)
                    if c < TT - 1:
                        dve.wait_ge(s_ps, nth(n, TT - 1, c))
                        if c == 0:
                            dve.tensor_copy(st[:, :], BS[:, 2 * P:3 * P]).then_inc(s_done, 1)
                        else:
                            dve.wait_ge(s_done, nth(n, TT - 1, c - 1))
                            dve.scalar_tensor_tensor(out=st[:, :], in0=st[:, :], scalar=hp[:, 5, c:c + 1],
                                                     in1=BS[:, 2 * P:3 * P], op0=ALU.mult, op1=ALU.add).then_inc(s_done, 1)

            def finish(n):
                h = n - 1
                dve.wait_ge(o_root, n)
                dve.reciprocal(T["L"][:, :], T["L"][:, :]).then_inc(o_inv, 1)
                dve.wait_ge(o_inv, n)
                dve.scalar_tensor_tensor(out=T["dm"][:, :], in0=BO[:, :], scalar=nrm[:, 0:1], in1=T["L"][:, :],
                                         op0=ALU.mult, op1=ALU.mult).then_inc(o_nrm, 1)
                dve.wait_ge(o_nrm, n)
                dve.tensor_tensor(mixT[:, bass.ds(h, 1), :].rearrange("p o s -> p (o s)"), T["dm"][:, :],
                                  T["sz"][:, :], ALU.mult).then_inc(o_done, 1)

            def iteration(it, gdn=True, last=False):
                if not last:
                    conv_weights(it)
                if gdn:
                    gdn0(it)
                    gdn1(it)
                if not last:
                    conv(it, 0)
                if gdn:
                    level(0, it)
                    level(1, it)
                if not last:
                    conv(it, 1)
                if gdn:
                    for l in range(2, LEVELS):
                        level(l, it)
                    scan(it)
                if not last:
                    conv(it, 2)
                if gdn:
                    finish(it)

            dve.wait_ge(cw_done, 1)
            dve.wait_ge(zero_pad, 5)
            dve.wait_ge(table_zero, 16)
            iteration(0, gdn=False)
            with dve.Fori(1, HEADS) as it:
                iteration(it)
            iteration(HEADS, last=True)

            def attend(m, j):
                u = 2 * m + j
                if j == 0:
                    W(dve, at_ps, 2 * m)
                    dve.tensor_copy(kg[:, :], kdup[:, bass.ds(m, 1), :].rearrange("p o s -> p (o s)"))
                    dve.tensor_copy(vg[:, :, :], vtok[:, :, bass.ds(m * HD, HD)])
                    dve.tensor_copy(sl[:, :, :], attn_small[:, :].rearrange("p (a h) -> p a h", a=2)[:, :, bass.ds(m * 4, 4)]).then_inc(at_small, 1)
                dve.wait_ge(at_small, m + 1)
                W(dve, pt_ps, 4 * u)
                for r in range(2):
                    for tp in range(2):
                        dve.wait_ge(sc_ps, 4 * u + (2 * r + tp + 1))
                        dve.scalar_tensor_tensor(out=sc[:, r, tp, :, :], in0=dist[:, tp:tp + 2, :],
                                                 scalar=sl[:, 0, 2 * j + r:2 * j + r + 1],
                                                 in1=[[B0, B1], [B2, BM]][r][tp][:, :].rearrange("p (a b) -> p a b", a=2),
                                                 op0=ALU.mult, op1=ALU.add).then_inc(sc_b, 1)
                        dve.wait_ge(sc_b, 4 * u + (2 * r + tp + 1))
                        dve.tensor_reduce(att8[:, 0, 4 * r + 2 * tp:4 * r + 2 * tp + 2], sc[:, r, tp, :, :], AX.X, ALU.max).then_inc(mx, 1)
                    dve.wait_ge(mx, 4 * u + (2 * r + 2))
                    dve.tensor_scalar(att8[:, 1, 4 * r:4 * r + 4], att8[:, 0, 4 * r:4 * r + 4],
                                      sl[:, 1, 2 * j + r:2 * j + r + 1], -1.0, ALU.max, ALU.mult).then_inc(nmx, 1)
                dve.wait_ge(pexp, u + 1)
                dve.tensor_tensor(att8[:, 4, :], att8[:, 2, :], att8[:, 3, :], ALU.add).then_inc(den, 1)
                dve.wait_ge(den, u + 1)
                dve.reciprocal(att8[:, 4, :], att8[:, 4, :]).then_inc(rec, 1)
                dve.wait_ge(rec, u + 1)
                for r in range(2):
                    for tp in range(2):
                        c = 4 * r + 2 * tp
                        dve.tensor_tensor(sc[:, r, tp, :, :], sc[:, r, tp, :, :],
                                          att8[:, 4, c:c + 2].rearrange("p (a o) -> p a o", o=1).broadcast_to([P, 2, 2 * P]),
                                          ALU.mult).then_inc(pn, 1)

            dve.wait_ge(v_tok, 2)
            dve.wait_ge(ld_att, 16)
            attend(0, 0)
            attend(0, 1)
            with dve.Fori(1, 3) as m:
                attend(m, 0)
                attend(m, 1)
            for i in range(3):
                dve.wait_ge(mix_hi, i + 1)
                dve.tensor_tensor(mxl[:, 4 * i:4 * i + 4, :], mixT[:, 4 * i:4 * i + 4, :],
                                  mxh[:, 4 * i:4 * i + 4, :].bitcast(F32), ALU.subtract).then_inc(mix_lo, 1)
            attend(3, 0)
            attend(3, 1)
            dve.wait_ge(mix_hi, 4)
            dve.tensor_tensor(mxl[:, 12:16, :], mixT[:, 12:16, :], mxh[:, 12:16, :].bitcast(F32),
                              ALU.subtract).then_inc(mix_lo, 1)

            dve.wait_ge(ld_h, 16)
            r1v = r1[:, :, :].rearrange("p t (n c) -> p t n c", c=S)
            with dve.Fori(0, 4) as nt:
                for t in range(TT):
                    if t < 3:
                        dve.wait_ge(y_ps, 3 * nt + (t + 1))
                    else:
                        dve.wait_ge(strip_mm, 4 * nt + (O0 + 4))
                    v = r1v[:, t, bass.ds(nt, 1), :].rearrange("p o c -> p (o c)")
                    dve.scalar_tensor_tensor(out=v, in0=v, scalar=ALPHA, in1=[B0, B1, B2, BM][t][:, :],
                                             op0=ALU.mult, op1=ALU.add).then_inc(y_out, 1)
                    dve.wait_ge(y_out, 4 * nt + (t + 1))
                    dve.bn_stats(bns4[:, t, bass.ds(nt, 1), :].rearrange("p o c -> p (o c)"), v).then_inc(l1_stats, 1)
            dve.wait_ge(l1_stats, 16)
            for t in range(TT):
                dve.bn_aggr(mv4[:, t, :], bns4[:, t, :, :].rearrange("p a b -> p (a b)")).then_inc(l1_step, 1)
            dve.wait_ge(l1_root, 1)
            dve.reciprocal(rs4[:, :], rs4[:, :]).then_inc(l1_step, 1)
            dve.wait_ge(l1_step, 5)
            dve.scalar_tensor_tensor(out=nm4[:, :], in0=mv4[:, :, 0:1].rearrange("p t o -> p (t o)"), scalar=-1.0,
                                     in1=rs4[:, :], op0=ALU.mult, op1=ALU.mult).then_inc(l1_step, 1)
            dve.wait_ge(ld_ln1, 80)
            for t in range(TT):
                dve.wait_ge(l1_norm, t + 1)
                dve.tensor_tensor(r1[:, t, :], r1[:, t, :], g1[:, :], ALU.mult).then_inc(l1_gain, 1)
                dve.wait_ge(l1_gain, t + 1)
                dve.tensor_tensor(r1[:, t, :], r1[:, t, :], b1[:, :], ALU.add).then_inc(h1_done, 1)

            k_ = [0]

            def step(i):
                k_[0] += 1
                i.then_inc(rt, 1)
                dve.wait_ge(rt, k_[0])

            def per(ap, width):
                return ap.rearrange("p (t o) -> p t o", o=1).broadcast_to([P, TT, width])

            def over_t(c0, c1):
                return rc[:, c0:c1].rearrange("p (o e) -> p o e", o=1).broadcast_to([P, TT, c1 - c0])

            dve.wait_ge(logits, 1)
            dve.wait_ge(h1_done, TT)
            step(dve.tensor_copy(lg[:, :, :], B0[:, 0:TT * 64].rearrange("p (t n) -> p t n", t=TT)[:, :, 0:GROUPS + E]))
            step(dve.tensor_reduce(gm[:, 0, :], lg[:, :, 0:GROUPS], AX.X, ALU.max))
            step(dve.tensor_tensor(ge[:, :, :], lg[:, :, 0:GROUPS], per(gm[:, 0, :], GROUPS), ALU.subtract))
            assert k_[0] == RT_GE
            step(dve.tensor_tensor(gsel[:, :, 0:GROUPS], lg[:, :, 0:GROUPS], per(gm[:, 0, :], GROUPS), ALU.is_equal))
            step(dve.scalar_tensor_tensor(out=gsel[:, :, 0:GROUPS], in0=gsel[:, :, 0:GROUPS], scalar=-8.0,
                                          in1=over_t(0, GROUPS), op0=ALU.mult, op1=ALU.add))
            step(dve.tensor_reduce(gm[:, 2, :], gsel[:, :, 0:GROUPS], AX.X, ALU.min))
            step(dve.tensor_scalar(gm[:, 2, :], gm[:, 2, :], 8.0, None, ALU.add))
            step(dve.tensor_tensor(gsel[:, :, :], over_t(2 * E, 3 * E), per(gm[:, 2, :], E), ALU.is_equal))
            step(dve.tensor_scalar(gsel[:, :, :], gsel[:, :, :], 1.0, -NEG, ALU.subtract, ALU.mult))
            step(dve.tensor_tensor(el[:, :, :], lg[:, :, GROUPS:], gsel[:, :, :], ALU.add))
            for t in range(TT):
                step(dve.max(top[:, t, :], el[:, t, :]))
                step(dve.max_index(topi[:, t, :], top[:, t, :], el[:, t, :]))
            step(dve.tensor_copy(topf[:, :, :], topi[:, :, 0:2]))
            step(dve.tensor_tensor(wts[:, 0, :], top[:, :, 1:2].rearrange("p t o -> p (t o)"),
                                   top[:, :, 0:1].rearrange("p t o -> p (t o)"), ALU.subtract))
            assert k_[0] == RT_D
            for c in range(2):
                step(dve.tensor_tensor(oh[:, c, :, :], over_t(0, E), topf[:, :, c:c + 1].broadcast_to([P, TT, E]), ALU.is_equal))
            step(dve.tensor_tensor(taken[:, :, :], oh[:, 0, :, :], oh[:, 1, :, :], ALU.add))
            assert k_[0] == RT_M
            dve.wait_ge(rt_exp, 2)
            step(dve.tensor_reduce(gm[:, 1, :], ge[:, :, :], AX.X, ALU.add))
            step(dve.reciprocal(gm[:, 3, :], gm[:, 1, :]))
            step(dve.tensor_scalar(wts[:, 2, :], wts[:, 1, :], 1.0, None, ALU.add))
            step(dve.reciprocal(wts[:, 2, :], wts[:, 2, :]))
            step(dve.tensor_tensor(wts[:, 2, :], wts[:, 2, :], gm[:, 3, :], ALU.mult))
            tok_w = toki[:, :, :, :].bitcast(F32)
            step(dve.tensor_copy(tok_w[:, :, 0:1, 1:2].rearrange("p t c o -> p (t c o)"), wts[:, 2, :]))
            step(dve.tensor_tensor(tok_w[:, :, 1:2, 1:2].rearrange("p t c o -> p (t c o)"), wts[:, 2, :], wts[:, 1, :], ALU.mult))
            dve.wait_ge(rt_ps, 1)
            pv = B1[:, 0:TT * E].rearrange("p (t e) -> p t e", t=TT)
            step(dve.tensor_tensor(el[:, :, :], pv, taken[:, :, :], ALU.subtract))
            step(dve.tensor_tensor(el[:, :, :], el[:, :, :], over_t(E, 2 * E), ALU.add))
            for c in range(2):
                step(dve.tensor_tensor(oh[:, c, :, :], oh[:, c, :, :], el[:, :, :], ALU.mult))
                step(dve.tensor_reduce(dstf[:, :, c:c + 1].rearrange("p t o -> p (t o)"), oh[:, c, :, :], AX.X, ALU.add))
            step(dve.tensor_copy(rd[:, :, :], dstf[:, :, :]))
            step(dve.tensor_copy(toki[:, :, :, 0:1].rearrange("p t c r -> p t (c r)"),
                                 rc[:, 3 * E:].rearrange("p (t o) -> p t o", o=1).broadcast_to([P, TT, 2])))
            assert k_[0] == RT_DEST
            nb, cum, one, cnt = (over_nb[:, i, :] for i in range(4))
            step(dve.tensor_copy(cnt, B1[:, TT * E:(TT + 1) * E]))
            step(dve.memset(one, 1.0))
            step(dve.memset(nb, 0.0))
            for b in range(1, CAP // SLOTS):
                step(dve.scalar_tensor_tensor(out=nb, in0=cnt, scalar=float(SLOTS * b), in1=nb, op0=ALU.is_gt, op1=ALU.add))
            step(dve.tensor_tensor_scan(cum, one, nb, 0.0, ALU.mult, ALU.add))
            item = rc[0:1, 0:LEFTOVER]
            item_e = item.rearrange("p (i o) -> p i o", o=1).broadcast_to([1, LEFTOVER, E])
            step(dve.tensor_tensor(ovc[:, :, :], over_nb[0:1, 1:2, :].broadcast_to([1, LEFTOVER, E]), item_e, ALU.is_le))
            step(dve.tensor_reduce(ovf[:, 0, :], ovc[:, :, :], AX.X, ALU.add))
            step(dve.tensor_tensor(ovp[:, :, :], ovc[:, :, :], over_nb[0:1, 0:1, :].broadcast_to([1, LEFTOVER, E]), ALU.mult))
            step(dve.tensor_reduce(ovf[:, 1, :], ovp[:, :, :], AX.X, ALU.add))
            step(dve.tensor_scalar(ovf[:, 0, :], ovf[:, 0, :], float(E - 1), None, ALU.min))
            step(dve.tensor_tensor(ovf[:, 2, :], item, ovf[:, 1, :], ALU.subtract))
            step(dve.tensor_scalar(ovf[:, 2, :], ovf[:, 2, :], 1.0, float(SLOTS), ALU.add, ALU.mult))
            step(dve.scalar_tensor_tensor(out=ovf[:, 2, :], in0=ovf[:, 0, :], scalar=float(CAP), in1=ovf[:, 2, :], op0=ALU.mult, op1=ALU.add))
            step(dve.tensor_scalar(ovf[:, 2, :], ovf[:, 2, :], float(E * CAP - SLOTS), None, ALU.min))
            step(dve.tensor_copy(ovi[:, 0:LEFTOVER], ovf[:, 0, :]))
            step(dve.tensor_copy(ovi[:, LEFTOVER:2 * LEFTOVER], ovf[:, 2, :]))
            step(dve.tensor_copy(ovi[:, 2 * LEFTOVER:], over_nb[0:1, 1, E - 1:E]))
            assert k_[0] == RT_ALL

            def add_rows(n, cs, by_tile=False, after=None):
                for c in cs:
                    tt, q = piece(c, by_tile)
                    dve.wait_ge(comb_ps, 4 * TT * n + (c + 1 - 4 * TT))
                    v = r1[:, tt, q * S:(q + 1) * S]
                    dve.tensor_tensor(v, v, [BS, BO][c % 2][:, :], ALU.add).then_inc(comb_done, 1)
                    if after:
                        after(c)

            def block_dve(t):
                dve.wait_ge(xT_ps, 2 * t + 2)
                W(dve, gu_used, 4 * t)
                dve.tensor_copy(xbT[:, 8:16, :], PA[1][:, :].rearrange("p (k n) -> p k n", k=8)).then_inc(xT_d, 1)
                dve.wait_ge(idx_loaded, 32 * t + 32)
                W(dve, yw_done, 4 * t)
                dve.tensor_copy(slot_tw[:, 0:1], idx[:, 0:1])
                dve.tensor_copy(slot_tw[:, 1:2], idx[:, 1:2].bitcast(F32)).then_inc(idx_read, 1)
                if not isinstance(t, int):
                    add_rows(t, range(0, BEFORE_HID))
                dve.wait_ge(sg_done, t + 1)
                dve.tensor_tensor(hid[SLOTS:P, :], hid[SLOTS:P, :], B0[SLOTS:P, :], ALU.mult).then_inc(hid_done, 1)
                if not isinstance(t, int):
                    add_rows(t, range(BEFORE_HID, 4 * TT))
                dve.wait_ge(idx_read, t + 1)
                dve.tensor_scalar(place[:, :], tokens[:, :], slot_tw[:, 0:1], None, ALU.is_equal).then_inc(placed_, 1)
                for q in range(4):
                    dve.wait_ge(yw_done, 4 * t + (q + 1))
                    dve.tensor_copy(yhl[:, q, :], yw[:, q, :]).then_inc(yw_hi, 1)
                    dve.wait_ge(yw_hi, 4 * t + (q + 1))
                    dve.tensor_tensor(yhl[SLOTS:P, q, :], yw[SLOTS:P, q, :], yhl[SLOTS:P, q, :].bitcast(F32),
                                      ALU.subtract).then_inc(yw_split, 1)

            block_dve(0)
            dve.wait_ge(scaled, TT)
            with dve.Fori(1, E) as t:
                block_dve(t)
            left = dve.value_load(ovi[0:1, 2 * LEFTOVER:2 * LEFTOVER + 1], min_val=0, max_val=LEFTOVER)
            with dve.If(left > 0):
                with dve.Fori(0, left) as i:
                    block_dve(i + E)
            dve.wait_ge(ld_ln2, 32)
            last = dve.snap(left + E)
            f = [0]

            def fstep(i):
                f[0] += 1
                i.then_inc(f_step, 1)
                dve.wait_ge(f_step, f[0])

            def stats(c):
                tt, q = divmod(c, 4)
                dve.wait_ge(comb_done, 4 * TT * last + (c + 1 - 4 * TT))
                fstep(dve.bn_stats(bns4[:, tt, q, :], r1[:, tt, q * S:(q + 1) * S]))
                if q == 3:
                    fstep(dve.bn_aggr(mv4[:, tt, :], bns4[:, tt, :, :].rearrange("p a b -> p (a b)")))
                    assert f[0] == f_var(tt)
                    if tt:
                        shift(tt - 1)

            def shift(t):
                dve.wait_ge(f_root, t + 1)
                fstep(dve.reciprocal(rs4[:, t:t + 1], rs4[:, t:t + 1]))
                fstep(dve.scalar_tensor_tensor(out=nm4[:, t:t + 1], in0=mv4[:, t, 0:1], scalar=-1.0,
                                               in1=rs4[:, t:t + 1], op0=ALU.mult, op1=ALU.mult))
                assert f[0] == f_bias(t)
                if t:
                    gain(t - 1)

            def gain(t):
                dve.wait_ge(f_norm, t + 1)
                dve.tensor_tensor(r1[:, t, :], r1[:, t, :], g2[:, :], ALU.mult).then_inc(f_gain, 1)

            add_rows(last, range(4 * TT), by_tile=True, after=stats)
            shift(TT - 1)
            gain(TT - 1)
            dve.wait_ge(f_gain, TT)
            dve.tensor_tensor(r1[:, TT - 1, :], r1[:, TT - 1, :], b2[:, :], ALU.add).then_inc(f_done, 1)

        @block.tensor
        def _(pe):
            mm = pe.matmul
            pe.wait_ge(ld_const, 16)
            for t in range(TT):
                pe.wait_ge(ln_step, LN_PER * (t + 1))
                for b in range(4):
                    W(pe, hT_lo, 4 * (t - 1) + b + 1)
                    for k in range(4):
                        i = pe.transpose(banks[4 + b][:, k * P:(k + 1) * P],
                                         xn[t % 2][:, (4 * b + k) * P:(4 * b + k + 1) * P], ident)
                    i.then_inc(hT_psum, 1)
            pe.wait_ge(ld_small, 16 * 7)
            pe.wait_ge(hT_lo, 4 * TT)
            pe.transpose(BM[:, 0:CONV * 24], cwraw[:, :], cst[0:CONV * 24, 0:CONV * 24]).then_inc(cw_psum, 1)

            def k_step(bank, hi_, lo_, rh, rl, first, final):
                mm(bank, lo_, rh, start=first, stop=False)
                mm(bank, hi_, rl, start=False, stop=False)
                return mm(bank, hi_, rh, start=False, stop=final)

            def k_steps(s, sl, k0, k1):
                for k in range(k0, k1):
                    if k == 0:
                        pe.wait_ge(strip_lo, s + 1)
                        W(pe, strip_out, s - 1)
                    i = k_step(PA[sl][:, :], whi[sl][:, k, :], wlo[sl][:, k, :], hTh[:, k, :], hTl[:, k, :],
                               k == 0, k == KD - 1)
                    if k == KD - 1:
                        i.then_inc(strip_mm, 1)

            k_steps(0, 0, 0, KD)
            pe.wait_ge(strip_out, 1)
            for c in range(TT):
                i = pe.transpose(B0[:, c * 2 * HEADS:(c + 1) * 2 * HEADS], bd[0:2 * HEADS, c * P:(c + 1) * P],
                                 cst[0:2 * HEADS, 0:2 * HEADS])
            i.then_inc(bd_T, 1)
            k_steps(1, 1, 0, KD)
            pe.wait_ge(bd_done, BD_G)
            g_all = wk[:, 1, :, :].rearrange("p c h -> p (c h)")
            mm(B0[:, 128:128 + TT * HEADS], tri, g_all, start=True, stop=True)
            mm(B0[:, 256:256 + TT * HEADS], ones, g_all, start=True, stop=True).then_inc(gcum, 1)

            def ch(name, c):
                return T[name][:, c * P:(c + 1) * P]

            def steps(it):
                done = [0]

                def feed(n):
                    for _ in range(n):
                        j, k = divmod(done[0], KD)
                        if j < 4:
                            k_steps(4 * it + 1 + j, slot(j), k, k + 1)
                            done[0] += 1
                return feed

            def gdn(n, feed):
                feed(4)
                for j in range(2):
                    pe.wait_ge(sq_done, nth(n, 2, j))
                    mm([B0, B1][j][:, :], ones, T[["dm", "L"][j]][:, :], start=True, stop=True).then_inc(ss_done, 1)
                pe.wait_ge(gb_ready, n)
                for c in range(TT):
                    i = mm(B2[:, c * P:(c + 1) * P], gb[:, c, :], tri, start=True, stop=True)
                i.then_inc(gc_row, 1)
                feed(12)
                pe.wait_ge(unit, 2 * n)
                for c in range(TT):
                    i = mm(B0[:, c * P:(c + 1) * P], ch("k", c), ch("k", c), start=True, stop=True)
                i.then_inc(gram, 1)
                for c in range(TT):
                    i = mm(B1[:, c * P:(c + 1) * P], ch("q", c), ch("k", c), start=True, stop=True)
                i.then_inc(qk, 1)
                feed(3)
                pe.wait_ge(exp_row, n)
                pe.wait_ge(diff, 4 * n)
                pe.wait_ge(L_done, n)
                for c in range(TT):
                    i = pe.transpose(B2[:, c * P:(c + 1) * P], ch("L", c), ident)
                i.then_inc(LT_ps, 1)
                pe.wait_ge(attn_done, n)
                for c in range(TT):
                    i = pe.transpose(BM[:, c * P:(c + 1) * P], ch("A", c), ident)
                i.then_inc(attnT_ps, 1)
                for c in range(TT):
                    i = pe.transpose(B0[:, c * P:(c + 1) * P], ch("v", c), ident)
                i.then_inc(v_ps, 1)
                for c in range(TT):
                    i = pe.transpose(B1[:, c * P:(c + 1) * P], ch("k", c), ident)
                i.then_inc(k_ps, 1)
                feed(4)
                pe.wait_ge(LT_done, n)
                pe.wait_ge(x_init, 4 * n)
                pe.wait_ge(vb_done, n)
                pe.wait_ge(kd_done, n)
                for l in range(LEVELS):
                    if l:
                        pe.wait_ge(xu, nth(n, LEVELS - 1, l - 1))
                    for c in range(TT):
                        i = mm(B0[:, c * P:(c + 1) * P], ch("LT", c), ch("X", c), start=True, stop=True)
                    i.then_inc(lx, 1)
                    feed(2)
                    pe.wait_ge(am, nth(n, LEVELS, l))
                    if l:
                        pe.wait_ge(xtu, nth(n, LEVELS, l - 1))
                    if l < LEVELS - 1:
                        for c in range(TT):
                            i = mm(B1[:, c * P:(c + 1) * P], ch("XT", c), ch("A", c), start=True, stop=True)
                        i.then_inc(xa, 1)
                    for c in range(TT):
                        i = mm(B2[:, c * P:(c + 1) * P], ch("A", c), ch("XT", c), start=True, stop=True)
                    i.then_inc(xat, 1)
                    feed(2)
                pe.wait_ge(attnT_done, n)
                pe.wait_ge(qd_done, n)
                pe.wait_ge(xtu, nth(n, LEVELS, LEVELS - 1))
                for c in range(TT):
                    if c:
                        pe.wait_ge(s_done, nth(n, TT - 1, c - 1))
                        mm(BS[:, 0:P], ch("k", c), st[:, :], start=True, stop=True).then_inc(ks, 1)
                        mm(BO[:, c * P:(c + 1) * P], st[:, :], ch("qd", c), start=True, stop=False)
                        feed(1)
                        pe.wait_ge(rr_done, nth(n, TT - 1, c - 1))
                    mm(BS[:, P:2 * P], ch("XT", c), rr[:, :] if c else ch("vb", c), start=True, stop=True).then_inc(vn_ps, 1)
                    feed(1)
                    pe.wait_ge(vn_done, nth(n, TT, c))
                    if c < TT - 1:
                        mm(BS[:, 2 * P:3 * P], ch("kd", c), vn[:, :], start=True, stop=True).then_inc(s_ps, 1)
                    i = mm(BO[:, c * P:(c + 1) * P], vn[:, :], ch("attnT", c), start=not c, stop=True)
                    feed(1)
                i.then_inc(o_ps, 1)
                feed(3)
                pe.wait_ge(o_sq, n)
                mm(BM[:, :], ones, T["A"][:, :], start=True, stop=True).then_inc(o_ss, 1)

            for j in range(1, 4):
                k_steps(1 + j, slot(j), 0, KD)
            with pe.Fori(1, HEADS) as it:
                feed = steps(it)
                pe.wait_ge(par_done, 1)
                gdn(it, feed)
                feed(4 * KD)
            feed = steps(HEADS)
            gdn(HEADS, feed)
            feed(4 * KD)

            for j in range(2):
                pe.wait_ge(strip_out, Q0 - 1 + j)
                pe.wait_ge(o_done, HEADS)
                for t in range(TT):
                    i = pe.transpose([B0, B1][j][:, t * P:(t + 1) * P], vT[:, j, t * P:(t + 1) * P], ident)
                i.then_inc(v_T, 1)
            for j in range(2):
                k_steps(Q0 + j, slot(j), 0, KD)

            def attend(m, j, feed):
                u = 2 * m + j
                feed(1)
                pe.wait_ge(at_small, m + 1)
                pe.wait_ge(strip_out, u + (Q0 + 1))
                W(pe, at_out, u)
                for r in range(2):
                    q0, q1 = HD * r, HD * (r + 1)
                    for tp in range(2):
                        for t in (2 * tp, 2 * tp + 1):
                            i = mm([[B0, B1], [B2, BM]][r][tp][:, (t % 2) * 2 * P:(t % 2 + 1) * 2 * P],
                                   aq[j][q0:q1, t * P:(t + 1) * P], kg[q0:q1, t * P:(t + 2) * P], start=True, stop=True)
                        i.then_inc(sc_ps, 1)
                feed(9)
                for r in range(2):
                    pe.wait_ge(pn, 4 * u + (2 * r + 2))
                    for g in range(2):
                        for t in range(TT):
                            i = pe.transpose([BS, BO, B0, B1][2 * r + g][:, t * P:(t + 1) * P],
                                             sc[:, r, t // 2, t % 2, g * P:(g + 1) * P], ident)
                        i.then_inc(pt_ps, 1)
                feed(3)
                pe.wait_ge(pt, 4 * u + 4)
                for r in range(2):
                    for t in range(TT):
                        o_ = B2[HD * r:HD * (r + 1), t * P:(t + 1) * P]
                        if t:
                            mm(o_, vg[:, t - 1, :], pT[:, 2 * r, t * P:(t + 1) * P], start=True, stop=False)
                        i = mm(o_, vg[:, t, :], pT[:, 2 * r + 1, t * P:(t + 1) * P], start=not t, stop=True)
                i.then_inc(at_ps, 1)
                feed(KD)

            def q_feed(m, j):
                done = [0]

                def feed(n):
                    for _ in range(n):
                        if done[0] < KD:
                            k_steps(2 * m + (Q0 + j), slot(j), done[0], done[0] + 1)
                            done[0] += 1
                return feed

            for j in range(2):
                attend(0, j, q_feed(1, j))
            with pe.Fori(2, 4) as m:
                for j in range(2):
                    attend(m - 1, j, q_feed(m, j))
            for j in range(2):
                attend(3, j, lambda n: None)

            def project(nt):
                for kg_ in range(4):
                    sl_ = slot(kg_)
                    wh = whi[sl_][:, :, :].rearrange("p (k a) n -> p k (a n)", k=4)
                    wl = wlo[sl_][:, :, :].rearrange("p (k a) n -> p k (a n)", k=4)
                    pe.wait_ge(strip_lo, 4 * nt + (O0 + 1 + kg_))
                    pe.wait_ge(mix_lo, kg_ + 1)
                    for t in range(TT):
                        if kg_ == 0:
                            W(pe, y_out, 4 * nt + (t - 3))
                        for k in range(4):
                            c = 4 * kg_ + k
                            i = k_step([B0, B1, B2, BM][t][:, :], mxh[:, c, t * P:(t + 1) * P], mxl[:, c, t * P:(t + 1) * P],
                                       wh[:, k, :], wl[:, k, :], c == 0, c == KD - 1)
                        if kg_ == 3 and t < 3:
                            i.then_inc(y_ps, 1)
                    i.then_inc(strip_mm, 1)

            pe.wait_ge(at_out, 8)
            project(0)
            with pe.Fori(1, 4) as nt:
                project(nt)

            for t in range(TT):
                pe.wait_ge(h1_done, t + 1)
                for b in range(4):
                    W(pe, h1T_done, 4 * (t - 1) + b + 1)
                    for k in range(4):
                        i = pe.transpose([PA[0], PA[1], BS, BO][b][:, k * P:(k + 1) * P],
                                         r1[:, t, (4 * b + k) * P:(4 * b + k + 1) * P], ident)
                    i.then_inc(h1T_ps, 1)
            pe.wait_ge(ld_ln1, 80)
            for t in range(TT):
                pe.wait_ge(h1T_done, 4 * t + 4)
                for k in range(KD):
                    i = mm(B0[:, t * 64:t * 64 + GROUPS + E], h1T[:, k, t * P:(t + 1) * P], wr[:, k, :], start=k == 0, stop=k == KD - 1)
            i.then_inc(logits, 1)
            pe.wait_ge(rt, RT_M)
            for t in range(TT):
                for t2 in range(t):
                    mm(B1[:, t * E:(t + 1) * E], ones, taken[:, t2, :], start=t2 == 0, stop=False)
                mm(B1[:, t * E:(t + 1) * E], tri, taken[:, t, :], start=t == 0, stop=True)
            for t in range(TT):
                i = mm(B1[:, TT * E:(TT + 1) * E], ones, taken[:, t, :], start=t == 0, stop=t == TT - 1)
            i.then_inc(rt_ps, 1)

            def combine(n, c, by_tile=False):
                tt, q = piece(c, by_tile)
                if c == 0:
                    pe.wait_ge(placed_, n)
                if c < 4 if by_tile else c % 4 == 0:
                    pe.wait_ge(yw_split, 4 * n + (q - 3))
                if c >= 2:
                    pe.wait_ge(comb_done, 4 * TT * n + (c - 1 - 4 * TT))
                mm([BS, BO][c % 2][:, :], place[:, tt * P:(tt + 1) * P], yhl[:, q, :],
                   start=True, stop=True).then_inc(comb_ps, 1)

            def block_pe(t):
                pe.wait_ge(gathered, 16 * t + 16)
                W(pe, xT_a, t)
                W(pe, xT_d, t)
                for g in range(2):
                    for k in range(8):
                        i = mm(PA[g][:, k * SLOTS:(k + 1) * SLOTS], xb[:, (8 * g + k) * P:(8 * g + k + 1) * P],
                               cst[0:SLOTS, 0:SLOTS], start=True, stop=True)
                    i.then_inc(xT_ps, 1)
                if isinstance(t, int):
                    pe.wait_ge(xT_a, t + 1)
                    pe.wait_ge(xT_d, t + 1)
                W(pe, hid_done, t)
                if not isinstance(t, int):
                    combine(t, 0)
                    combine(t, 1)
                    pe.wait_ge(xT_a, t + 1)
                    pe.wait_ge(xT_d, t + 1)
                for kg_ in range(4):
                    pe.wait_ge(gu_loaded[kg_], 32 * t + 32)
                    for k in range(4):
                        c = 4 * kg_ + k
                        for h in range(2):
                            i = mm(B0[SLOTS * h:SLOTS * (h + 1), :], xbT[:, c, :], wpiece[2 * kg_ + h][:, k * F:(k + 1) * F],
                                   start=c == 0, stop=c == KD - 1)
                        if k == 3:
                            i.then_inc(gu_used, 1)
                        if not isinstance(t, int) and 2 <= c < BEFORE_HID:
                            combine(t, c)
                if not isinstance(t, int):
                    combine(t, BEFORE_HID)
                    combine(t, BEFORE_HID + 1)
                W(pe, hidT_done, t)
                pe.wait_ge(hid_done, t + 1)
                for c in range(KF):
                    i = mm(B1[:, c * SLOTS:(c + 1) * SLOTS], hid[SLOTS:P, c * P:(c + 1) * P],
                           cst[SLOTS:P, K_ID + SLOTS:K_ID + P], start=True, stop=True)
                i.then_inc(hT_ps, 1)
                W(pe, yw_done, 4 * t)
                if not isinstance(t, int):
                    for c in range(BEFORE_HID + 2, 4 * TT):
                        combine(t, c)
                pe.wait_ge(hidT_done, t + 1)
                for c in range(KF):
                    pe.wait_ge(dn_loaded[c], 16 * t + 16)
                    for j in range(2):
                        for h in range(2):
                            n0 = (2 * j + h) * F
                            i = mm([B2, BM][j][SLOTS * h:SLOTS * (h + 1), :], hidT[:, c, :], wpiece[8 + c][:, n0:n0 + F],
                                   start=c == 0, stop=c == KF - 1)
                    i.then_inc(dn_used, 1)

            block_pe(0)
            with pe.Fori(1, E) as t:
                block_pe(t)
            pe.wait_ge(rt, RT_ALL)
            left = pe.value_load(ovi[0:1, 2 * LEFTOVER:2 * LEFTOVER + 1], min_val=0, max_val=LEFTOVER)
            with pe.If(left > 0):
                with pe.Fori(0, left) as i:
                    block_pe(i + E)
            last = pe.snap(left + E)
            for c in range(4 * TT):
                combine(last, c, by_tile=True)


_INS = ["x", "ln0_g", "ln0_b", "w_in", "conv_w", "a_log", "dt_bias", "gdn_norm_w", "sinks", "w_o", "ln1_g", "ln1_b",
        "w_route_group", "w_route_expert", "w_gate", "w_up", "w_down", "ln2_g", "ln2_b"]


def kernel(**inputs):
    import concourse.bacc as bacc
    from concourse.bass_utils import run_bass_kernel_spmd

    nc = bacc.Bacc("TRN2", target_bir_lowering=False, num_devices=1)
    given = {name: np.ascontiguousarray(inputs[name]) for name in _INS}
    given |= dict(zip(("consts", "att_consts", "route_consts"), shape_constants()))
    arrays, args = {}, []
    for name, a in given.items():
        arrays[f"in_{name}"] = a
        args.append(nc.dram_tensor(f"in_{name}", a.shape, mybir.dt.from_np(a.dtype), kind="ExternalInput").ap())
    args.append(nc.dram_tensor("out", (1, S, D), F32, kind="ExternalOutput").ap())
    build(nc, *args)
    r = run_bass_kernel_spmd(nc, [arrays], core_ids=[0])
    return r.results[0]["out"]
```

```python
from contextlib import ExitStack

import numpy as np

import concourse.bass as bass
from concourse import mybir

ALU = mybir.AluOpType
ACT = mybir.ActivationFunctionType
F32 = mybir.dt.float32
F32R = mybir.dt.float32r
I32 = mybir.dt.int32
AX = mybir.AxisListType

P = 128
D = 2048
S = 512
TT = S // P
KD = D // P
HEADS = 8
DK = 128
CONV = 4
QH, KVH, HD = 16, 4, 64
CHUNK = 64
A_QKV = 3 * HEADS * DK
C_BETA = 4 * HEADS * DK
C_BQ = C_BETA + 2 * HEADS
C_BK = C_BQ + QH * HD
C_BV = C_BK + KVH * HD
IN_COLS = C_BV + KVH * HD
GROUPS, PER_GROUP = 4, 8
E = GROUPS * PER_GROUP
F = 512
KF = F // P
SLOTS = 64
CAP = S
LEFTOVER = S * 2 // SLOTS
ALPHA = 2.0 ** 0.25
LN_EPS, RMS_EPS = 1e-5, 1e-6
NEG = -1.0e30

STRIPS = 1 + 4 * (HEADS + 1) + 8
PIECES = 16
LEVELS = 6

K_ID = 0
K_TRI = K_ID + P
K_ONE = K_TRI + P
K_M1T = K_ONE + P
K_MASK = K_M1T + P
K_END = K_MASK + 7 * P
J_DIST = 0
J_SLOPE = J_DIST + 3 * 2 * P
J_END = J_SLOPE + QH


def shape_constants():
    i = np.arange(P)[:, None]
    j = np.arange(P)[None, :]
    k = np.zeros((P, K_END), np.float32)
    k[:, K_ID:K_ID + P] = i == j
    k[:, K_TRI:K_TRI + P] = i <= j
    k[:, K_ONE:K_ONE + P] = 1.0
    for l in range(7):
        b = 1 << l
        m = (i // (2 * b) == j // (2 * b)) & (i % (2 * b) >= b) & (j % (2 * b) < b)
        k[:, K_MASK + l * P:K_MASK + (l + 1) * P] = m
        if l == 0:
            k[:, K_M1T:K_M1T + P] = m.T
    a = np.zeros((P, J_END), np.float32)
    key = np.arange(2 * P)[None, :] - P
    seen = (key // CHUNK >= i // CHUNK - 1) & (key // CHUNK <= i // CHUNK)
    dist = np.where(seen, np.abs(i - key), -NEG).astype(np.float32)
    first = np.where(key >= 0, dist, np.float32(-NEG))
    a[:, 0:2 * P] = first
    a[:, 2 * P:4 * P] = dist
    a[:, 4 * P:6 * P] = dist
    a[:, J_SLOPE:J_END] = -(2.0 ** (-8.0 * np.arange(1, QH + 1) / QH))[None, :]
    r = np.zeros((P, 3 * E + TT + S), np.float32)
    r[:, 0:E] = np.arange(E)[None, :]
    r[:, E:2 * E] = (np.arange(E) * CAP)[None, :]
    r[:, 2 * E:3 * E] = np.arange(E)[None, :] // PER_GROUP
    r[:, 3 * E:3 * E + TT] = np.arange(TT)[None, :] * P + i
    r[:, 3 * E + TT:] = np.arange(S)[None, :]
    return k, a, r


def build(nc, x, ln0_g, ln0_b, w_in, conv_w, a_log, dt_bias, gdn_norm_w, sinks, w_o, ln1_g, ln1_b,
          w_route_group, w_route_expert, w_gate, w_up, w_down, ln2_g, ln2_b, consts, att_consts,
          route_consts, out):
    x2 = x[0].rearrange("(t p) d -> p t d", p=P)
    out2 = out[0].rearrange("(t p) d -> p t d", p=P)
    w_in_v = w_in[0].rearrange("(k p) n -> p k n", p=P)
    w_o_v = w_o[0].rearrange("(k p) n -> p k n", p=P)
    gate_v = w_gate[0].rearrange("e (k p) f -> p e k f", p=P)
    up_v = w_up[0].rearrange("e (k p) f -> p e k f", p=P)
    down_v = w_down[0].rearrange("e (c p) n -> p e c n", p=P)

    ctx = ExitStack()
    with ctx:
        def sem(name):
            return ctx.enter_context(nc.semaphore(name))

        def dram(name, shape, dt):
            return nc.dram_tensor(name, shape, dt).ap()

        h_scr = dram("h_scr", (S, D), F32)
        h1_scr = dram("h1_scr", (S, D), F32)
        slot_rows = dram("slot_rows", (E * CAP, 2), I32)
        h_scr_v = h_scr.rearrange("(t p) d -> p t d", p=P)
        h1_scr_v = h1_scr.rearrange("(t p) d -> p t d", p=P)

        ARENA = 212000
        arena = ctx.enter_context(nc.sbuf_tensor("arena", [P, ARENA // 4], F32))
        base = nc.sbuf_base - ARENA
        placed = {}

        def at(name, offset, shape, dt=F32):
            size = 4 * int(np.prod(shape[1:]))
            assert offset + size <= ARENA, (name, offset + size)
            placed[name] = offset + size
            return nc.alloc_sbuf_tensor_at(name, list(shape), dt, offset=base + offset)

        KB = 1024
        HT, ST, MX, GD, CN = 0, 64 * KB, 112 * KB, 144 * KB, 198 * KB
        hTh = at("hTh", HT, [P, KD, S], F32R)
        hTl = at("hTl", HT + 32 * KB, [P, KD, S], F32R)
        raw = [at(f"raw{i}", ST + 8 * KB * i, [P, KD * P]) for i in range(2)]
        whi = [at(f"whi{i}", ST + 8 * KB * (2 + i), [P, KD, P], F32R) for i in range(2)]
        wlo = [at(f"wlo{i}", ST + 8 * KB * (4 + i), [P, KD, P], F32R) for i in range(2)]
        mixT = at("mixT", MX, [P, KD, S])
        xt = [at(f"xt{t}", GD + 8 * KB * t, [P, D]) for t in range(TT)]
        gb_rows = at("gb_rows", GD + 32 * KB, [2 * KD, P])
        gbT = at("gbT", GD + 33 * KB, [P, 2 * KD])
        g0 = at("g0", GD + 36 * KB, [P, D])
        b0 = at("b0", GD + 44 * KB, [P, D])
        hv = [at(f"hv{i}", MX + 2 * KB * (1 + i), [P, S]) for i in range(4)]
        o = GD
        xp = [at(f"xp{j}", o + 2112 * j, [P, S + CONV]) for j in range(3)]
        o += 2112 * 3
        half = [at(f"half{j}", o + 2 * KB * j, [P, S]) for j in range(4)]
        o += 8 * KB
        th = [at(f"th{j}", o + 2 * KB * j, [P, S]) for j in range(4)]
        o += 8 * KB
        ATT = o
        names = ["q", "k", "v", "dm", "L", "X", "XT", "qd", "Ed", "LT", "attnT", "vb", "kd", "A", "sz"]
        T = {}
        for n in names:
            T[n] = at("gd_" + n, o, [P, S])
            o += 2 * KB
        vn = at("vn", o, [P, P]); o += 512
        rr = at("rr", o, [P, P]); o += 512
        st = at("st", o, [P, P]); o += 512
        assert o <= CN, o
        kdup = at("kdup", GD, [P, KVH, S + P])
        vT = at("vT", GD + 10 * KB, [P, 2, S])
        vtok = at("vtok", GD + 14 * KB, [P, TT, KVH * HD])
        dist = at("dist", GD + 18 * KB, [P, 3, 2 * P])
        aq = [at(f"aq{i}", ATT + 2 * KB * i, [P, S]) for i in range(4)]
        sc = at("sc", ATT + 8 * KB, [P, 2, 2, 2, 2 * P])
        pT = at("pT", ATT + 16 * KB, [P, 4, S])
        kg = at("kg", ATT + 24 * KB, [P, S + P])
        vg = at("vg", ATT + 24 * KB + 2560, [P, TT, HD])
        sl = at("sl", ATT + 24 * KB + 2560 + 1024, [P, 2, 4])
        mxh = at("mxh", HT, [P, KD, S], F32R)
        mxl = at("mxl", HT + 32 * KB, [P, KD, S], F32R)
        r1 = at("r1", MX, [P, TT, D])
        g1 = at("g1", GD, [P, D])
        b1 = at("b1", GD + 8 * KB, [P, D])
        h1T = at("h1T", GD + 16 * KB, [P, KD, S])
        wr = at("wr", GD + 48 * KB, [P, KD, GROUPS + E])
        wpiece = [at(f"wpiece{i}", HT + 8 * KB * i, [P, 4 * F]) for i in range(12)]
        xb = at("xb", GD + 16 * KB, [SLOTS, D])
        yw = at("yw", GD + 24 * KB, [P, 4, F])
        yhl = at("yhl", GD + 32 * KB, [P, 4, F], F32R)
        xbT = at("xbT", GD + 40 * KB, [P, KD, SLOTS])
        hid = at("hid", GD + 48 * KB, [P, F])
        hidT = at("hidT", GD + 44 * KB, [P, KF, SLOTS])
        place = at("place", GD + 45 * KB, [P, S], F32R)
        tokens = at("tokens", GD + 51 * KB, [P, S])
        g2 = at("g2", HT + 96 * KB, [P, D])
        b2 = at("b2", HT + 104 * KB, [P, D])
        o = CN
        small = {}

        def keep(name, shape, dt=F32):
            nonlocal o
            t = at(name, o, shape, dt)
            o += (4 * int(np.prod(shape[1:])) + 31) // 32 * 32
            return t

        cst = keep("cst", [P, K_END])
        rc = keep("rc", [P, 3 * E + TT])
        attn_small = keep("attn_small", [P, 2 * QH])
        cw = keep("cw", [P, CONV * 24])
        cwraw = at("cwraw", GD + 52 * KB, [CONV * 24, P])
        cwh = keep("cwh", [P, CONV, 3])
        eps = keep("eps", [P, 2])
        nrm = keep("nrm", [P, 1])
        bns4 = keep("bns4", [P, TT, 4, 6])
        mv4 = keep("mv4", [P, TT, 2])
        rs4 = keep("rs4", [P, TT])
        nm4 = keep("nm4", [P, TT])
        tokpar = keep("tokpar", [P, HEADS, 6, TT])
        hp = keep("hp", [P, 6, TT])
        gb = at("gb", ATT + 2 * KB * names.index("A"), [P, TT, P])
        bd = at("bd", MX + 10 * KB, [P, S])
        ab = keep("ab", [P, 2, HEADS])
        bdt = at("bdt", ATT + 2 * KB * names.index("kd"), [P, TT, 2 * HEADS])
        att8 = keep("att8", [P, 5, 8])
        wk = at("wk", ATT + 2 * KB * names.index("vb"), [P, 6, TT, HEADS])
        slot_tw = keep("slot_tw", [P, 2])
        rd = keep("rd", [P, TT, 2], I32)
        idx = keep("idx", [P, 2], I32)
        idx_all = at("idx_all", GD + 47 * KB, [P, E + 1, 2], I32)
        ovi = keep("ovi", [1, 2 * LEFTOVER + 1], I32)
        o2_ = [GD]

        def scratch(name, shape, dt=F32):
            t = at(name, o2_[0], shape, dt)
            o2_[0] += (4 * int(np.prod(shape[1:])) + 31) // 32 * 32
            return t

        lgT = scratch("lgT", [P, S])
        lg = scratch("lg", [P, TT, GROUPS + E])
        gm = scratch("gm", [P, 4, TT])
        ge = scratch("ge", [P, TT, GROUPS])
        gsel = scratch("gsel", [P, TT, E])
        el = scratch("el", [P, TT, E])
        top = scratch("top", [P, TT, 8])
        topi = scratch("topi", [P, TT, 8], mybir.dt.uint32)
        topf = scratch("topf", [P, TT, 2])
        oh = scratch("oh", [P, 2, TT, E])
        taken = scratch("taken", [P, TT, E])
        tile_sums = scratch("tile_sums", [P, TT, E])
        dstf = scratch("dstf", [P, TT, 2])
        wts = scratch("wts", [P, 4, TT])
        over_nb = scratch("over_nb", [P, 4, E])
        ovc = scratch("ovc", [1, LEFTOVER, E])
        ovp = scratch("ovp", [1, LEFTOVER, E])
        ovf = scratch("ovf", [1, 4, LEFTOVER])
        toki = scratch("toki", [P, TT, 2, 2], I32)
        assert o2_[0] <= GD + 16 * KB
        unused = at("unused", MX, [P, 2 * E * CAP // P], I32)
        ident = cst[:, K_ID:K_ID + P]
        tri = cst[:, K_TRI:K_TRI + P]
        ones = cst[:, K_ONE:K_ONE + P]

        banks = [ctx.enter_context(nc.psum_tensor(f"bank{i}", [P, S], F32)) for i in range(8)]
        PA = banks[0:2]
        B0, B1, B2, BM, BS, BO = banks[2:8]

        TB = banks[2:8]

        ld_const = sem("ld_const"); ld_small = sem("ld_small"); ld_x = [sem(f"ld_x{t}") for t in range(TT)]
        ld_gb = sem("ld_gb"); ld_g0 = sem("ld_g0"); raw_loaded = [sem(f"raw_loaded{i}") for i in range(2)]
        ld_att = sem("ld_att")
        ln_step = sem("ln_step"); ln_sqrt = sem("ln_sqrt")
        small_T = sem("small_T"); gbT_done = sem("gbT_done"); hv_done = sem("hv_done"); h_done = sem("h_done")
        ln_norm = sem("ln_norm")
        h_stored = sem("h_stored")
        hT_psum = sem("hT_psum"); hT_hi = sem("hT_hi"); hT_lo = sem("hT_lo")
        strip_hi = sem("strip_hi"); strip_lo = sem("strip_lo"); strip_mm = sem("strip_mm"); strip_out = sem("strip_out")

        zero_pad = sem("zero_pad"); cw_done = sem("cw_done")
        bd_done = sem("bd_done"); bda = sem("bda"); gcum = sem("gcum")
        par_done = sem("par_done")
        kpad = sem("kpad")
        taps = sem("taps")
        conv_w_ready = sem("conv_w_ready")
        tanh_done = sem("tanh_done")
        silu = [sem(f"silu{j}") for j in range(4)]
        hp_ready = sem("hp_ready"); gb_ready = sem("gb_ready")
        sq_done = sem("sq_done")
        ss_done = sem("ss_done")
        root = sem("root")
        inv = sem("inv")
        unit = sem("unit")
        gc_row = sem("gc_row"); exp_row = sem("exp_row"); diff = sem("diff"); dec_exp = sem("dec_exp"); dec = sem("dec")
        qd_done = sem("qd_done")
        gram = sem("gram"); qk = sem("qk"); L_done = sem("L_done"); attn_done = sem("attn_done")
        LT_ps = sem("LT_ps"); attnT_ps = sem("attnT_ps"); vk_ps = sem("vk_ps")
        LT_done = sem("LT_done"); attnT_done = sem("attnT_done"); vb_done = sem("vb_done"); kd_done = sem("kd_done")
        x_init = sem("x_init")
        lx = sem("lx"); am = sem("am"); xat = sem("xat"); xtu = sem("xtu")
        xa = sem("xa"); xu = sem("xu")
        vn_ps = sem("vn_ps"); vn_done = sem("vn_done")
        ks = sem("ks"); rr_done = sem("rr_done"); s_ps = sem("s_ps"); s_done = sem("s_done")
        o_ps = sem("o_ps"); o_sq = sem("o_sq"); o_ss = sem("o_ss"); o_root = sem("o_root"); o_inv = sem("o_inv")
        o_nrm = sem("o_nrm"); o_done = sem("o_done")

        v_T = sem("v_T"); v_tok = sem("v_tok"); at_small = sem("at_small")
        sc_ps = sem("sc_ps"); sc_b = sem("sc_b"); mx = sem("mx"); nmx = sem("nmx"); pexp = sem("pexp")
        inv_sum = sem("inv_sum"); pn = sem("pn"); pt_ps = sem("pt_ps"); pt = sem("pt")
        at_ps = sem("at_ps"); at_out = sem("at_out")
        mix_hi = sem("mix_hi"); mix_lo = sem("mix_lo"); ld_h = sem("ld_h"); y_ps = sem("y_ps"); y_out = sem("y_out")
        ld_ln1 = sem("ld_ln1"); l1_step = sem("l1_step"); l1_root = sem("l1_root")
        l1_norm = sem("l1_norm"); l1_gain = sem("l1_gain"); h1_last = sem("h1_last"); lgT_done = sem("lgT_done"); h1_done = sem("h1_done"); h1_stored = sem("h1_stored")
        h1T_ps = sem("h1T_ps"); h1T_done = sem("h1T_done"); logits = sem("logits")
        rt = sem("rt"); rt_exp = sem("rt_exp"); rt_ps = sem("rt_ps"); table_zeroed = sem("table_zeroed"); table_zero = sem("table_zero")
        scattered = sem("scattered")
        gu_loaded = [sem(f"gu_loaded{i}") for i in range(4)]; dn_loaded = [sem(f"dn_loaded{i}") for i in range(4)]
        idx_loaded = sem("idx_loaded"); idx_read = sem("idx_read"); idx_next = sem("idx_next"); placed_ = sem("placed"); gathered = sem("gathered"); xT_ps = sem("xT_ps"); xT_a = sem("xT_a"); xT_d = sem("xT_d")
        gu_used = sem("gu_used"); sg_done = sem("sg_done"); hid_done = sem("hid_done"); hT_ps = sem("hT_ps")
        hidT_done = sem("hidT_done"); dn_used = sem("dn_used"); dn_half = sem("dn_half"); yw_done = sem("yw_done"); yw_hi = sem("yw_hi"); yw_split = sem("yw_split"); comb_ps = sem("comb_ps"); comb_done = sem("comb_done"); scaled = sem("scaled")
        ld_ln2 = sem("ld_ln2")
        f_step = sem("f_step"); f_root = sem("f_root"); f_gain = sem("f_gain"); f_done = sem("f_done"); f_done_p = sem("f_done_p")
        out_stored = sem("out_stored")

        Q0 = 1 + 4 * (HEADS + 1)
        O0 = STRIPS

        def W(eng, s, n):
            if not (isinstance(n, int) and n <= 0):
                eng.wait_ge(s, n)

        RT_GE, RT_D, RT_M = 4, 21, 24
        RT_DEST = RT_M + 7 + 2 + 5 + 4 + 2
        RT_ALL = RT_DEST + 3 + (CAP // SLOTS - 1) + 1 + 12
        F_VAR = 4 * TT + TT
        POOL_TILES, DVE_TILES = (0, 1), (3, 2)

        BEFORE_HID = 12

        def piece(c):
            return divmod(c, TT)[::-1]

        def nth(n, per, k):
            return n * per + (k + 1 - per)

        def slot(j):
            return (1 + j) % 2

        def loads(it, j):
            return 16 * (2 * it + (1 + j) // 2 + 1)

        def ln_var(t):
            return 5 * (t + 1) + 2 * max(t - 1, 0)

        def ln_bias(t):
            return ln_var(min(t + 1, TT - 1)) + 2 * (1 + (t == TT - 1))

        def l1_var(t):
            return 2 * (t + 1) + 2 * max(t - 1, 0)

        def l1_bias(t):
            return l1_var(min(t + 1, TT - 1)) + 2 * (1 + (t == TT - 1))

        BD_E, BD_G, BD_GC = 6, 15, 18

        block = ctx.enter_context(nc.Block())

        @block.sync
        def _(sp):
            for t in range(2):
                sp.dma_start(xt[t][:, :], x2[:, t, :]).then_inc(ld_x[t], 16)
            sp.dma_start(cst[:, :], consts).then_inc(ld_const, 16)
            for t in range(2, TT):
                sp.dma_start(xt[t][:, :], x2[:, t, :]).then_inc(ld_x[t], 16)
            sp.dma_start(gb_rows[0:KD, :], ln0_g.rearrange("(k p) -> k p", p=P)).then_inc(ld_gb, 16)
            sp.dma_start(gb_rows[KD:, :], ln0_b.rearrange("(k p) -> k p", p=P)).then_inc(ld_gb, 16)
            sp.dma_start(raw[0][:, :].rearrange("p (k n) -> p k n", k=KD),
                         w_in_v[:, :, C_BETA:C_BETA + P]).then_inc(raw_loaded[0], 16)
            sp.dma_start(rc[:, :], route_consts[:, 0:3 * E + TT]).then_inc(ld_small, 16)
            sp.dma_start(cwraw[:, :], conv_w[0].rearrange("a (c p) -> (a c) p", p=P)).then_inc(ld_small, 16)
            sp.dma_start(ab[:, 0, :], a_log[0].partition_broadcast(P)).then_inc(ld_small, 16)
            sp.dma_start(ab[:, 1, :], dt_bias[0].partition_broadcast(P)).then_inc(ld_small, 16)
            sp.dma_start(nrm[:, :], gdn_norm_w[0].rearrange("(p o) -> p o", o=1)).then_inc(ld_small, 16)
            sp.dma_start(attn_small[:, QH:], sinks[0].partition_broadcast(P)).then_inc(ld_small, 16)
            sp.dma_start(attn_small[:, 0:QH], att_consts[:, J_SLOPE:J_END]).then_inc(ld_small, 16)

            def strip_loads(it, cols, js=range(4)):
                for j in js:
                    W(sp, strip_lo, 4 * it + j)
                    sp.dma_start(raw[slot(j)][:, :].rearrange("p (k n) -> p k n", k=KD),
                                 cols(j)).then_inc(raw_loaded[slot(j)], 16)

            def head_cols(it):
                return lambda j: w_in_v[:, :, bass.ds(it * P + j * HEADS * DK, P)]

            strip_loads(0, head_cols(0), js=[0])
            sp.dma_start(g0[:, :], ln0_g.partition_broadcast(P)).then_inc(ld_g0, 16)
            sp.dma_start(b0[:, :], ln0_b.partition_broadcast(P)).then_inc(ld_g0, 16)
            strip_loads(0, head_cols(0), js=[1, 2])
            for t in range(TT):
                sp.wait_ge(h_done, 2 * t + 2)
                sp.dma_start(h_scr_v[:, t, :], xt[t][:, :]).then_inc(h_stored, 16)
            strip_loads(0, head_cols(0), js=[3])
            with sp.Fori(1, HEADS) as it:
                strip_loads(it, head_cols(it))
            strip_loads(HEADS, lambda j: w_in_v[:, :, C_BK + P * j:C_BK + P * (j + 1)])
            sp.wait_ge(silu[2], HEADS)
            sp.wait_ge(silu[3], HEADS)
            sp.dma_start(dist[:, :, :], att_consts[:, 0:6 * P].rearrange("p (a b) -> p a b", a=3)).then_inc(ld_att, 16)

            def ring_load(s_, sl_, src, k):
                W(sp, strip_lo, s_ - 1)
                sp.dma_start(raw[sl_][:, :].rearrange("p (k n) -> p k n", k=k), src).then_inc(raw_loaded[sl_], 16)

            with sp.Fori(0, 4) as m:
                for j in range(2):
                    ring_load(2 * m + (Q0 + j), slot(j), w_in_v[:, :, bass.ds(m * (2 * P) + (C_BQ + P * j), P)], KD)
            def o_loads(nt):
                for kg_ in range(4):
                    ring_load(4 * nt + (O0 + kg_), slot(kg_),
                              w_o_v[:, 4 * kg_:4 * kg_ + 4, bass.ds(nt * S, S)], 4)

            o_loads(0)
            sp.wait_ge(mix_lo, 4)
            sp.wait_ge(h_stored, 16 * TT)
            sp.dma_start(r1[:, :, :], h_scr_v).then_inc(ld_h, 16)
            sp.dma_start(g1[:, :], ln1_g[0].partition_broadcast(P)).then_inc(ld_ln1, 16)
            sp.dma_start(b1[:, :], ln1_b[0].partition_broadcast(P)).then_inc(ld_ln1, 16)
            sp.dma_start(tokens[:, :], route_consts[:, 3 * E + TT:]).then_inc(ld_ln1, 16)
            sp.dma_start(wr[:, :, 0:GROUPS], w_route_group[0].rearrange("(k p) n -> p k n", p=P)).then_inc(ld_ln1, 16)
            sp.dma_start(wr[:, :, GROUPS:], w_route_expert[0].rearrange("(k p) n -> p k n", p=P)).then_inc(ld_ln1, 16)
            with sp.Fori(1, 4) as nt:
                o_loads(nt)
            sp.wait_ge(strip_mm, STRIPS + PIECES)
            sp.dma_start(g2[:, :], ln2_g[0].partition_broadcast(P)).then_inc(ld_ln2, 16)
            sp.dma_start(b2[:, :], ln2_b[0].partition_broadcast(P)).then_inc(ld_ln2, 16)

            def expert_weights(t, e):
                for i in range(12):
                    if i < 8:
                        W(sp, gu_used, 4 * t + (i // 2 - 3))
                        src = [gate_v, up_v][i % 2][:, bass.ds(e, 1), 4 * (i // 2):4 * (i // 2) + 4, :]
                        sp.dma_start(wpiece[i][:, :].rearrange("p (k f) -> p k f", k=4),
                                     src.rearrange("p o k f -> p (o k) f")).then_inc(gu_loaded[i // 2], 16)
                    else:
                        W(sp, dn_used, 4 * t + (i - 8 - 3))
                        src = down_v[:, bass.ds(e, 1), i - 8:i - 7, :]
                        sp.dma_start(wpiece[i][:, :], src.rearrange("p o c n -> p (o c n)")).then_inc(dn_loaded[i - 8], 16)

            expert_weights(0, 0)
            with sp.Fori(1, E) as t:
                expert_weights(t, t)
            sp.wait_ge(rt, RT_ALL)
            left = sp.value_load(ovi[0:1, 2 * LEFTOVER:2 * LEFTOVER + 1], min_val=0, max_val=LEFTOVER)
            with sp.If(left > 0):
                with sp.Fori(0, left) as i:
                    e = sp.value_load(ovi[0:1, bass.ds(i, 1)], min_val=0, max_val=E - 1)
                    expert_weights(i + E, e)
            for i in range(2):
                for tiles_, done in ((POOL_TILES, f_done_p), (DVE_TILES, f_done)):
                    sp.wait_ge(done, i + 1)
                    sp.dma_start(out2[:, tiles_[i], :], r1[:, tiles_[i], :]).then_inc(out_stored, 16)
            sp.wait_ge(out_stored, 16 * TT)

        @block.gpsimd
        def _(pool):
            pool.memset(unused[:, :], 0).then_inc(table_zeroed, 1)
            pool.wait_ge(table_zeroed, 1)
            pool.dma_start(slot_rows.rearrange("(p n) o -> p (n o)", p=P), unused[:, :]).then_inc(table_zero, 16)
            pool.memset(eps[:, 0:1], LN_EPS).then_inc(zero_pad, 1)
            pool.memset(eps[:, 1:2], RMS_EPS).then_inc(zero_pad, 1)
            def lo(s, sl):
                pool.wait_ge(strip_hi, s + 1)
                W(pool, strip_mm, s - 1)
                pool.tensor_tensor(wlo[sl][:, :, :].rearrange("p k n -> p (k n)"), raw[sl][:, :],
                                   whi[sl][:, :, :].rearrange("p k n -> p (k n)").bitcast(F32),
                                   ALU.subtract).then_inc(strip_lo, 1)

            lo(0, 0)
            lo(1, 1)

            def iteration(it, gdn=True, last=False):
                for j in range(4):
                    lo(4 * it + 2 + j, slot(j + 1))
                    if j == 1 and not gdn:
                        pool.wait_ge(h_stored, 16 * TT)
                        for i in range(3):
                            pool.memset(xp[i][:, 0:CONV - 1], 0.0).then_inc(zero_pad, 1)
                    if j == 0 and gdn:
                        pool.wait_ge(par_done, 1)
                        pool.wait_ge(dec_exp, it)
                        ed = T["Ed"][:, :].rearrange("p (c i) -> p c i", c=TT)
                        pool.affine_select(out=ed, in_=ed, compare_op=ALU.is_ge, fill=0.0, base=0,
                                           pattern=[[0, TT], [-1, P]], channel_multiplier=1).then_inc(dec, 1)
                        if last:
                            for i in range(3):
                                pool.wait_ge(silu[i], HEADS)
                            pool.memset(kdup[:, :, 0:P], 0.0).then_inc(kpad, 1)

            iteration(0, gdn=False)
            with pool.Fori(1, HEADS) as it:
                iteration(it)
            iteration(HEADS, last=True)
            with pool.Fori(0, 4) as m:
                for j in range(2):
                    lo(2 * m + (Q0 + 1 + j), j)
            with pool.Fori(0, 3) as nt:
                for kg_ in range(4):
                    lo(4 * nt + (O0 + 1 + kg_), kg_ % 2)
            for kg_ in range(3):
                lo(O0 + 13 + kg_, kg_ % 2)
            pool.wait_ge(ld_ln1, 80)
            pool.wait_ge(l1_norm, TT)
            pool.tensor_tensor(r1[:, TT - 1, :], r1[:, TT - 1, :], g1[:, :], ALU.mult).then_inc(h1_last, 1)
            pool.wait_ge(h1_last, 1)
            pool.tensor_tensor(r1[:, TT - 1, :], r1[:, TT - 1, :], b1[:, :], ALU.add).then_inc(h1_last, 1)
            pool.wait_ge(table_zero, 16)
            pool.wait_ge(rt, RT_DEST)
            for t in range(TT):
                for c in range(2):
                    pool.indirect_dma_start(slot_rows, bass.IndirectOffsetOnAxis(ap=rd[:, t, c:c + 1], axis=0),
                                            toki[:, t, c, :], None).then_inc(scattered, 16)
            pool.wait_ge(scattered, 16 * 2 * TT)
            pool.wait_ge(rt, RT_ALL)
            pool.wait_ge(logits, 2)
            pool.wait_ge(h1_stored, 16 * TT)
            r_idx, r_free = pool.alloc_register("r_idx"), pool.alloc_register("r_free")

            def load_idx(row):
                for h in range(2):
                    pool.dma_start(idx[SLOTS * h:SLOTS * (h + 1), :], slot_rows[bass.ds(row, SLOTS), :]).then_inc(idx_loaded, 16)

            def gather(t, ready, count):
                pool.reg_mov(r_idx, count)
                pool.reg_mov(r_free, 2 * t)
                pool.wait_ge(h1_stored, 16 * TT)
                pool.wait_ge(ready, r_idx)
                if not isinstance(t, int):
                    pool.wait_ge(xT_ps, r_free)
                pool.indirect_dma_start(xb[:, :], None, h1_scr,
                                        bass.IndirectOffsetOnAxis(ap=idx[0:SLOTS, 0:1], axis=0)).then_inc(gathered, 16)

            load_idx(0)
            gather(0, idx_loaded, 32)
            for h in range(2):
                pool.dma_start(idx_all[SLOTS * h:SLOTS * (h + 1), 0:E, :],
                               slot_rows.rearrange("(e c) o -> c e o", c=CAP)[0:SLOTS, :, :]).then_inc(scattered, 16)
            pool.memset(idx_all[:, E:, :], 0).then_inc(table_zeroed, 1)
            with pool.Fori(1, E) as t:
                gather(t, idx_next, t)
            left = pool.value_load(ovi[0:1, 2 * LEFTOVER:2 * LEFTOVER + 1], min_val=0, max_val=LEFTOVER)
            with pool.If(left > 0):
                with pool.Fori(0, left) as i:
                    row = pool.value_load(ovi[0:1, bass.ds(i + LEFTOVER, 1)], min_val=0, max_val=E * CAP - SLOTS)
                    pool.wait_ge(gathered, 16 * i + 16 * E)
                    pool.wait_ge(idx_read, i + E)
                    pool.wait_ge(idx_next, E)
                    load_idx(row)
                    gather(i + E, idx_loaded, 32 * i + 64)
            pool.wait_ge(ld_ln2, 32)
            for i, t in enumerate(POOL_TILES):
                pool.wait_ge(f_root, 2 + i)
                pool.tensor_tensor(r1[:, t, :], r1[:, t, :], b2[:, :], ALU.add).then_inc(f_done_p, 1)

        @block.scalar
        def _(act):
            def copy(o_, i_, s, scale=1.0):
                return act.activation(o_, i_, ACT.Copy, scale=scale).then_inc(s, 1)

            act.wait_ge(zero_pad, 2)
            for t in range(TT):
                act.wait_ge(ln_step, ln_var(t))
                act.activation(rs4[:, t:t + 1], mv4[:, t, 1:2], ACT.Sqrt, bias=eps[:, 0:1]).then_inc(ln_sqrt, 1)
                act.wait_ge(ln_step, ln_bias(t))
                act.activation(xt[t][:, :], xt[t][:, :], ACT.Identity, bias=nm4[:, t:t + 1],
                               scale=rs4[:, t:t + 1]).then_inc(ln_norm, 1)

            act.wait_ge(gbT_done, 1)

            def h_out(k):
                act.wait_ge(hT_psum, k + 1)
                W(act, hT_lo, k - 3)
                act.activation(hv[k % 4][:, :], TB[k % 6][:, :], ACT.Identity, bias=gbT[:, KD + k:KD + k + 1],
                               scale=gbT[:, k:k + 1]).then_inc(hv_done, 1)

            def hi(s, sl, landed):
                act.wait_ge(raw_loaded[sl], landed)
                W(act, strip_mm, s - 1)
                act.activation(whi[sl][:, :, :].rearrange("p k n -> p (k n)"), raw[sl][:, :],
                               ACT.Copy).then_inc(strip_hi, 1)

            def hi_half(s, sl, landed, i):
                act.wait_ge(raw_loaded[sl], landed)
                act.wait_ge(strip_mm, s - 1)
                ks_ = slice(i * KD // 2, (i + 1) * KD // 2)
                a = act.activation(whi[sl][:, ks_, :].rearrange("p k n -> p (k n)"),
                                   raw[sl][:, i * KD * P // 2:(i + 1) * KD * P // 2], ACT.Copy)
                if i:
                    a.then_inc(strip_hi, 1)

            for k in range(6):
                h_out(k)
            hi(0, 0, 16)
            for k in range(6, KD):
                h_out(k)
            hi(1, 1, 16)
            act.wait_ge(strip_mm, 1)
            act.activation(bd[:, :], PA[0][:, :], ACT.Copy).then_inc(strip_out, 1)
            def out_qkv(it, j):
                act.wait_ge(strip_mm, 4 * it + 2 + j)
                if isinstance(it, int) and j == 0:
                    act.wait_ge(h_stored, 16 * TT)
                W(act, taps, 3 * CONV * it + CONV * (j - 2) if not isinstance(it, int) or it else 0)
                act.activation(xp[j][:, CONV - 1:CONV - 1 + S], PA[slot(j)][:, :], ACT.Copy).then_inc(strip_out, 1)

            def out_z(it):
                act.wait_ge(strip_mm, 4 * it + 5)
                act.activation(half[3][:, :], PA[0][:, :], ACT.Copy, scale=0.5)
                act.activation(th[3][:, :], PA[0][:, :], ACT.Tanh, scale=0.5).then_inc(strip_out, 1)

            def tanh(it, j):
                act.wait_ge(taps, 3 * CONV * it + CONV * (j + 1))
                W(act, silu[j], it)
                act.activation(th[j][:, :], half[j][:, :], ACT.Tanh).then_inc(tanh_done, 1)

            def gdn0(n):
                for j in range(2):
                    act.wait_ge(silu[j], n)
                    act.activation(T[["dm", "L"][j]][:, :], T[["q", "k"][j]][:, :], ACT.Square).then_inc(sq_done, 1)
                for j in range(2):
                    act.wait_ge(ss_done, nth(n, 2, j))
                    act.activation(T[["X", "XT"][j]][:, :], [B0, B1][j][:, :], ACT.Sqrt, bias=eps[:, 1:2]).then_inc(root, 1)
                act.wait_ge(gc_row, n)
                act.activation(T["qd"][:, :], B2[:, :], ACT.Exp).then_inc(exp_row, 1)
                act.wait_ge(diff, 4 * n)
                act.activation(T["Ed"][:, :], T["dm"][:, :], ACT.Exp, scale=-1.0).then_inc(dec_exp, 1)

            def gdn1(n):
                act.wait_ge(LT_ps, n)
                act.activation(T["LT"][:, :], B2[:, :], ACT.Copy).then_inc(LT_done, 1)
                act.wait_ge(attnT_ps, n)
                act.activation(T["attnT"][:, :], BM[:, :], ACT.Copy).then_inc(attnT_done, 1)

            def gdn3(n, between):
                for c in range(TT):
                    act.wait_ge(vn_ps, nth(n, TT, c))
                    act.activation(vn[:, :], BS[:, P:2 * P], ACT.Copy).then_inc(vn_done, 1)
                    between(c)
                act.wait_ge(o_ps, n)
                act.activation(T["A"][:, :], BO[:, :], ACT.Square).then_inc(o_sq, 1)
                act.wait_ge(o_ss, n)
                act.activation(T["L"][:, :], BM[:, :], ACT.Sqrt, bias=eps[:, 1:2], scale=1.0 / DK).then_inc(o_root, 1)

            def next_hi(it, j):
                hi(4 * it + 2 + j, slot(j + 1), loads(it, j + 1))

            def iteration(it, gdn=True, last=False):
                next_hi(it, 0)
                if gdn:
                    out_z(it - 1)
                    gdn0(it)
                next_hi(it, 1)
                out_k(0) if last else out_qkv(it, 0)
                if gdn:
                    gdn1(it)
                if not last:
                    tanh(it, 0)
                next_hi(it, 2)
                out_k(1) if last else out_qkv(it, 1)
                if not last:
                    tanh(it, 1)

                def between(c):
                    if c < 2:
                        hi_half(4 * it + 5, slot(4), loads(it, 4), c)
                    elif c == TT - 1:
                        out_v(0) if last else out_qkv(it, 2)

                gdn3(it, between)
                if not last:
                    tanh(it, 2)

            def out_k(j):
                act.wait_ge(strip_mm, 4 * HEADS + 2 + j)
                if j == 0:
                    for i in range(3):
                        act.wait_ge(silu[i], HEADS)
                    act.wait_ge(kpad, 1)
                for g in range(2):
                    for r in range(2):
                        i = act.activation(kdup[HD * r:HD * (r + 1), 2 * j + g, P:P + S],
                                           PA[slot(j)][HD * g:HD * (g + 1), :], ACT.Copy)
                i.then_inc(strip_out, 1)

            def out_v(j):
                act.wait_ge(strip_mm, 4 * HEADS + 4 + j)
                act.wait_ge(silu[3], HEADS)
                act.activation(vT[:, j, :], PA[slot(j + 2)][:, :], ACT.Copy).then_inc(strip_out, 1)

            def beta_decay():
                act.wait_ge(bd_done, 3)
                act.activation(wk[:, 0, :, :], wk[:, 0, :, :], ACT.Exp, scale=-1.0).then_inc(bda, 1)
                act.activation(ab[:, 0, :], ab[:, 0, :], ACT.Exp).then_inc(bda, 1)
                act.activation(wk[:, 2, :, :], wk[:, 1, :, :], ACT.Abs).then_inc(bda, 1)
                act.wait_ge(bda, 3)
                act.activation(wk[:, 2, :, :], wk[:, 2, :, :], ACT.Exp, scale=-1.0).then_inc(bda, 1)
                act.wait_ge(bd_done, BD_E)
                act.activation(wk[:, 4, :, :], wk[:, 3, :, :], ACT.Ln).then_inc(bda, 1)

            def cumulated_decay():
                act.wait_ge(bd_done, BD_GC)
                act.activation(wk[:, 3, :, :], wk[:, 2, :, :], ACT.Exp).then_inc(bda, 1)
                act.activation(wk[:, 4, :, :], wk[:, 4, :, :], ACT.Exp).then_inc(bda, 1)
                act.activation(wk[:, 5, :, :], wk[:, 5, :, :], ACT.Exp).then_inc(bda, 1)

            next_hi(0, 0)
            next_hi(0, 1)
            out_qkv(0, 0)
            beta_decay()
            next_hi(0, 2)
            out_qkv(0, 1)
            cumulated_decay()
            out_qkv(0, 2)
            next_hi(0, 3)
            for j in range(3):
                tanh(0, j)
            with act.Fori(1, HEADS) as it:
                iteration(it)
            iteration(HEADS, last=True)

            def attend(m, j):
                u = 2 * m + j
                for r in range(2):
                    act.wait_ge(nmx, 2 * u + (r + 1))
                    act.activation(att8[:, 3, 4 * r:4 * r + 4], att8[:, 1, 4 * r:4 * r + 4], ACT.Exp,
                                   bias=sl[:, 1, 2 * j + r:2 * j + r + 1])
                    for t in range(TT):
                        v = sc[:, r, t // 2, t % 2, :]
                        i = act.activation(v, v, ACT.Exp, bias=att8[:, 1, 4 * r + t:4 * r + t + 1],
                                           accum_out=att8[:, 2, 4 * r + t:4 * r + t + 1])
                i.then_inc(pexp, 1)
                for i in range(4):
                    act.wait_ge(pt_ps, 4 * u + (i + 1))
                    act.activation(pT[:, i, :], [BS, BO, B0, B1][i][:, :], ACT.Copy).then_inc(pt, 1)
                act.wait_ge(at_ps, u + 1)
                act.activation(mixT[:, bass.ds(u + HEADS, 1), :].rearrange("p o s -> p (o s)"), B2[:, :],
                               ACT.Copy).then_inc(at_out, 1)

            def out_q(u, j):
                act.wait_ge(strip_mm, u + (Q0 + 1))
                act.activation(aq[j][:, :], PA[slot(j)][:, :], ACT.Copy, scale=float(HD) ** -0.5).then_inc(strip_out, 1)

            def q_hi(m, j):
                hi(2 * m + (Q0 + 1 + j), j, 16 * m + 16 * ((Q0 + 1) // 2 + 1))

            q_hi(0, 0)
            out_v(1)
            for j in range(2):
                act.wait_ge(v_T, j + 1)
                act.activation(vtok[:, :, P * j:P * (j + 1)],
                               [B0, B1][j][:, :].rearrange("p (t n) -> p t n", t=TT), ACT.Copy).then_inc(v_tok, 1)
            act.wait_ge(o_done, HEADS)
            q_hi(0, 1)
            out_q(0, 0)
            with act.Fori(1, 4) as m:
                q_hi(m, 0)
                out_q(2 * m - 1, 1)
                attend(m - 1, 0)
                q_hi(m, 1)
                out_q(2 * m, 0)
                attend(m - 1, 1)
            q_hi(4, 0)
            out_q(7, 1)

            def split_mix(i):
                act.activation(mxh[:, 4 * i:4 * i + 4, :], mixT[:, 4 * i:4 * i + 4, :], ACT.Copy).then_inc(mix_hi, 1)

            attend(3, 0)
            act.wait_ge(strip_mm, STRIPS)
            act.wait_ge(at_out, 4)
            split_mix(0)
            attend(3, 1)
            for i in range(1, 3):
                split_mix(i)
            act.wait_ge(at_out, 8)
            split_mix(3)

            def o_hi(nt, kg_):
                hi(4 * nt + (O0 + 1 + kg_), kg_ % 2, 32 * nt + 16 * ((O0 + 1 + kg_) // 2 + 1))

            for kg_ in range(1, 4):
                o_hi(0, kg_)
            with act.Fori(1, 3) as nt:
                for kg_ in range(4):
                    o_hi(nt, kg_)
            for kg_ in range(3):
                o_hi(3, kg_)

            for t in range(TT):
                act.wait_ge(l1_step, l1_var(t))
                act.activation(rs4[:, t:t + 1], mv4[:, t, 1:2], ACT.Sqrt, bias=eps[:, 0:1]).then_inc(l1_root, 1)
                act.wait_ge(l1_step, l1_bias(t))
                act.activation(r1[:, t, :], r1[:, t, :], ACT.Identity, bias=nm4[:, t:t + 1], scale=rs4[:, t:t + 1]).then_inc(l1_norm, 1)
            for t in range(TT):
                if t < TT - 1:
                    act.wait_ge(h1_done, t + 1)
                else:
                    act.wait_ge(h1_last, 2)
                act.dma_start(h1_scr_v[:, t, :], r1[:, t, :]).then_inc(h1_stored, 16)
                for b in range(4):
                    act.wait_ge(h1T_ps, 4 * t + b + 1)
                    act.activation(h1T[:, 4 * b:4 * b + 4, t * P:(t + 1) * P],
                                   [PA[0], PA[1], BS, BO][b][:, :].rearrange("p (k n) -> p k n", k=4), ACT.Copy).then_inc(h1T_done, 1)
            act.wait_ge(logits, 1)
            for r in (0, SLOTS):
                i = act.activation(lgT[r:r + GROUPS + E, :], B0[r:r + GROUPS + E, :], ACT.Copy)
            i.then_inc(lgT_done, 1)
            act.wait_ge(rt, RT_GE)
            act.activation(ge[:, :, :], ge[:, :, :], ACT.Exp).then_inc(rt_exp, 1)
            act.wait_ge(rt, RT_D)
            act.activation(wts[:, 1, :], wts[:, 0, :], ACT.Exp).then_inc(rt_exp, 1)

            def block_act(t):
                act.wait_ge(xT_ps, 2 * t + 1)
                W(act, gu_used, 4 * t)
                act.activation(xbT[:, 0:8, :], PA[0][:, :].rearrange("p (k n) -> p k n", k=8), ACT.Copy).then_inc(xT_a, 1)
                act.wait_ge(gu_used, 4 * t + 4)
                W(act, hT_ps, t)
                act.activation(hid[SLOTS:P, :], B0[0:SLOTS, :], ACT.Silu).then_inc(sg_done, 1)
                act.wait_ge(hT_ps, t + 1)
                W(act, dn_used, 4 * t)
                act.activation(hidT[:, :, :], B1[:, 0:KF * SLOTS].rearrange("p (c n) -> p c n", c=KF), ACT.Copy).then_inc(hidT_done, 1)
                act.wait_ge(dn_half, t + 1)
                act.wait_ge(idx_read, t + 1)
                W(act, yw_split, 4 * t)
                for q in range(4):
                    j, h = divmod(q, 2)
                    if q == 2:
                        act.wait_ge(dn_used, 4 * t + 4)
                    for o_ in range(2):
                        half_ = slice(SLOTS * o_, SLOTS * (o_ + 1))
                        i = act.activation(yw[half_, q, :], [B2, BM][j][SLOTS * h:SLOTS * (h + 1), :], ACT.Copy,
                                           scale=slot_tw[half_, 1:2])
                    i.then_inc(yw_done, 1)

            act.wait_ge(h1_stored, 16 * TT)
            act.wait_ge(h1T_ps, 4 * TT)
            for t in range(TT):
                act.activation(r1[:, t, :], r1[:, t, :], ACT.Copy, scale=ALPHA).then_inc(scaled, 1)
            act.wait_ge(rt, RT_ALL)
            block_act(0)
            with act.Fori(1, E) as t:
                block_act(t)
            left = act.value_load(ovi[0:1, 2 * LEFTOVER:2 * LEFTOVER + 1], min_val=0, max_val=LEFTOVER)
            with act.If(left > 0):
                with act.Fori(0, left) as i:
                    block_act(i + E)
            act.wait_ge(f_step, F_VAR)
            act.activation(rs4[:, :], mv4[:, :, 1:2].rearrange("p t o -> p (t o)"), ACT.Sqrt, bias=eps[:, 0:1]).then_inc(f_root, 1)
            act.wait_ge(f_step, F_VAR + 1)
            for t in POOL_TILES:
                act.wait_ge(f_gain, t + 1)
                act.activation(r1[:, t, :], r1[:, t, :], ACT.Copy, scale=rs4[:, t:t + 1]).then_inc(f_root, 1)

        @block.vector
        def _(dve):
            n_ln = [0]

            def ln_(i):
                n_ln[0] += 1
                i.then_inc(ln_step, 1)
                dve.wait_ge(ln_step, n_ln[0])

            def ln_shift(t):
                dve.wait_ge(ln_sqrt, t + 1)
                ln_(dve.reciprocal(rs4[:, t:t + 1], rs4[:, t:t + 1]))
                ln_(dve.scalar_tensor_tensor(out=nm4[:, t:t + 1], in0=mv4[:, t, 0:1], scalar=-1.0, in1=rs4[:, t:t + 1],
                                             op0=ALU.mult, op1=ALU.mult))
                assert n_ln[0] == ln_bias(t)

            for t in range(TT):
                dve.wait_ge(ld_x[t], 16)
                for q in range(4):
                    ln_(dve.bn_stats(bns4[:, t, q, :], xt[t][:, q * S:(q + 1) * S]))
                ln_(dve.bn_aggr(mv4[:, t, :], bns4[:, t, :, :].rearrange("p a b -> p (a b)")))
                assert n_ln[0] == ln_var(t)
                if t:
                    ln_shift(t - 1)
            ln_shift(TT - 1)
            dve.wait_ge(small_T, 1)
            dve.tensor_copy(gbT[:, :], TB[5][:, 0:2 * KD]).then_inc(gbT_done, 1)
            for k in range(KD):
                dve.wait_ge(hv_done, k + 1)
                dve.tensor_copy(hTh[:, k, :], hv[k % 4][:, :]).then_inc(hT_hi, 1)
                dve.wait_ge(hT_hi, k + 1)
                dve.tensor_tensor(hTl[:, k, :], hv[k % 4][:, :], hTh[:, k, :].bitcast(F32), ALU.subtract).then_inc(hT_lo, 1)
            dve.wait_ge(ld_g0, 32)
            dve.wait_ge(hT_psum, KD)
            for t in range(TT):
                dve.tensor_tensor(xt[t][:, :], xt[t][:, :], g0[:, :], ALU.mult).then_inc(h_done, 1)
                dve.wait_ge(h_done, 2 * t + 1)
                dve.tensor_tensor(xt[t][:, :], xt[t][:, :], b0[:, :], ALU.add).then_inc(h_done, 1)
            dve.wait_ge(small_T, 2)
            dve.tensor_copy(cw[:, :], BM[:, 0:CONV * 24]).then_inc(cw_done, 1)
            dve.wait_ge(small_T, 3)
            dve.wait_ge(h_done, 2 * TT)
            pv = B0[:, 0:TT * 2 * HEADS].rearrange("p (c n) -> p c n", c=TT)
            dve.tensor_copy(bdt[:, :, :], pv).then_inc(bd_done, 1)
            dve.wait_ge(bd_done, 1)
            dve.wait_ge(ld_small, 16 * 7)
            dve.tensor_copy(wk[:, 0, :, :], bdt[:, :, 0:HEADS]).then_inc(bd_done, 1)
            dve.tensor_tensor(wk[:, 1, :, :], bdt[:, :, HEADS:], ab[:, 1:2, :].broadcast_to([P, TT, HEADS]),
                              ALU.add).then_inc(bd_done, 1)
            dve.wait_ge(bda, 4)
            n = [3]

            def link(i):
                n[0] += 1
                i.then_inc(bd_done, 1)
                dve.wait_ge(bd_done, n[0])

            w_ = lambda i: wk[:, i, :, :]
            link(dve.tensor_scalar(w_(0), w_(0), 1.0, None, ALU.add))
            link(dve.reciprocal(w_(0), w_(0)))
            link(dve.tensor_scalar(w_(3), w_(2), 1.0, None, ALU.add))
            link(dve.tensor_scalar(w_(5), w_(3), 1.0, None, ALU.is_equal))
            link(dve.tensor_tensor(w_(5), w_(5), w_(2), ALU.mult))
            dve.wait_ge(bda, 5)
            link(dve.tensor_scalar(w_(3), w_(3), 1.0, 1e-30, ALU.subtract, ALU.max))
            link(dve.reciprocal(w_(3), w_(3)))
            link(dve.tensor_tensor(w_(3), w_(3), w_(2), ALU.mult))
            link(dve.tensor_tensor(w_(3), w_(3), w_(4), ALU.mult))
            link(dve.tensor_tensor(w_(3), w_(3), w_(5), ALU.add))
            link(dve.scalar_tensor_tensor(out=w_(3), in0=w_(1), scalar=0.0, in1=w_(3), op0=ALU.max, op1=ALU.add))
            link(dve.scalar_tensor_tensor(out=w_(1), in0=w_(3), scalar=-1.0,
                                          in1=ab[:, 0:1, :].broadcast_to([P, TT, HEADS]), op0=ALU.mult, op1=ALU.mult))
            assert n[0] == BD_G
            dve.wait_ge(gcum, 1)
            gcv = B0[:, 128:128 + TT * HEADS].rearrange("p (c n) -> p c n", c=TT)
            glv = B0[:, 256:256 + TT * HEADS].rearrange("p (c n) -> p c n", c=TT)
            link(dve.tensor_copy(w_(2), gcv))
            link(dve.tensor_copy(w_(5), glv))
            link(dve.tensor_tensor(w_(4), w_(5), w_(2), ALU.subtract))
            tp = lambda i: tokpar[:, :, i, :].rearrange("p h c -> p c h")
            link(dve.tensor_copy(tp(0), w_(1)))
            link(dve.tensor_copy(tp(1), w_(0)))
            link(dve.tensor_copy(tp(2), w_(2)))
            dve.wait_ge(bda, 8)
            link(dve.scalar_tensor_tensor(out=tp(3), in0=w_(0), scalar=-1.0, in1=w_(3), op0=ALU.mult, op1=ALU.mult))
            link(dve.tensor_copy(tp(4), w_(4)))
            dve.tensor_copy(tp(5), w_(5)).then_inc(par_done, 1)

            def conv(it, j, steps=range(CONV)):
                for a in steps:
                    if a == 0:
                        dve.wait_ge(strip_out, 4 * it + 2 + j)
                        dve.wait_ge(conv_w_ready, it + 1)
                        W(dve, silu[j], it)
                        dve.tensor_scalar(half[j][:, :], xp[j][:, 0:S], cwh[:, 0, j:j + 1], None, ALU.mult).then_inc(taps, 1)
                        continue
                    dve.wait_ge(taps, 3 * CONV * it + (CONV * j + a))
                    dve.scalar_tensor_tensor(out=half[j][:, :], in0=xp[j][:, a:a + S], scalar=cwh[:, a, j:j + 1],
                                             in1=half[j][:, :], op0=ALU.mult, op1=ALU.add).then_inc(taps, 1)

            def conv_weights(it):
                W(dve, taps, 3 * CONV * it)
                view = cw[:, :].rearrange("p (a j h) -> p h a j", a=CONV, j=3)
                dve.tensor_scalar(cwh[:, :, :], view[:, bass.ds(it, 1), :, :].rearrange("p o a j -> p (o a) j"), 0.5,
                                  None, ALU.mult).then_inc(conv_w_ready, 1)

            def act_silu(j, n):
                if j < 3:
                    dve.wait_ge(tanh_done, nth(n, 3, j))
                else:
                    dve.wait_ge(strip_out, 4 * n + 1)
                dve.scalar_tensor_tensor(out=T[["q", "k", "v", "sz"][j]][:, :], in0=th[j][:, :], scalar=1.0,
                                         in1=half[j][:, :], op0=ALU.add, op1=ALU.mult).then_inc(silu[j], 1)

            def tiles(name):
                return T[name][:, :].rearrange("p (c i) -> p c i", c=TT)

            def psum_tiles(b):
                return b[:, :].rearrange("p (c i) -> p c i", c=TT)

            def over(col):
                return hp[:, col, :].rearrange("p (c o) -> p c o", o=1).broadcast_to([P, TT, P])

            def mask(l):
                return cst[:, K_MASK + l * P:K_MASK + (l + 1) * P].rearrange("p (o i) -> p o i", o=1).broadcast_to([P, TT, P])

            def wide(c0):
                return cst[:, c0:c0 + P].rearrange("p (o i) -> p o i", o=1).broadcast_to([P, TT, P])

            def gdn0(n):
                h = n - 1
                act_silu(0, n)
                act_silu(1, n)
                dve.tensor_copy(hp[:, :, :].rearrange("p f c -> p (f c)"),
                                tokpar[:, bass.ds(h, 1), :, :].rearrange("p o f c -> p (o f c)")).then_inc(hp_ready, 1)
                dve.wait_ge(hp_ready, n)
                dve.tensor_copy(gb[:, :, :], over(0)).then_inc(gb_ready, 1)
                act_silu(2, n)
                act_silu(3, n)
                for j in range(2):
                    dve.wait_ge(root, nth(n, 2, j))
                    t_ = T[["X", "XT"][j]]
                    dve.reciprocal(t_[:, :], t_[:, :]).then_inc(inv, 1)
                dve.wait_ge(exp_row, n)
                dve.wait_ge(ss_done, nth(n, 2, 0))
                for c in range(TT):
                    dve.tensor_scalar(tiles("dm")[:, c, :], B2[:, c * P:(c + 1) * P], hp[:, 2, c:c + 1], 0.0,
                                      ALU.subtract, ALU.max).then_inc(diff, 1)
                dve.wait_ge(inv, nth(n, 2, 0))
                dve.scalar_tensor_tensor(out=T["q"][:, :], in0=T["q"][:, :], scalar=float(DK) ** -0.5, in1=T["X"][:, :],
                                         op0=ALU.mult, op1=ALU.mult).then_inc(unit, 1)
                dve.wait_ge(inv, nth(n, 2, 1))
                dve.tensor_tensor(T["k"][:, :], T["k"][:, :], T["XT"][:, :], ALU.mult).then_inc(unit, 1)
                dve.wait_ge(exp_row, n)
                dve.wait_ge(unit, nth(n, 2, 0))
                dve.tensor_tensor(T["qd"][:, :], T["qd"][:, :], T["q"][:, :], ALU.mult).then_inc(qd_done, 1)

            def gdn1(n):
                dve.wait_ge(dec, n)
                dve.wait_ge(gram, n)
                for c in range(TT):
                    i = dve.scalar_tensor_tensor(out=tiles("L")[:, c, :], in0=B0[:, c * P:(c + 1) * P],
                                                 scalar=hp[:, 1, c:c + 1], in1=tiles("Ed")[:, c, :],
                                                 op0=ALU.mult, op1=ALU.mult)
                i.then_inc(L_done, 1)
                dve.wait_ge(qk, n)
                dve.wait_ge(gc_row, n)
                dve.tensor_tensor(T["A"][:, :], B1[:, :], T["Ed"][:, :], ALU.mult).then_inc(attn_done, 1)
                dve.wait_ge(L_done, n)
                dve.wait_ge(unit, 2 * n)
                dve.tensor_tensor(tiles("X"), tiles("L"), mask(0), ALU.mult).then_inc(x_init, 1)
                dve.wait_ge(x_init, nth(n, 4, 0))
                dve.tensor_tensor(tiles("X"), wide(K_ID), tiles("X"), ALU.subtract).then_inc(x_init, 1)
                dve.wait_ge(LT_done, n)
                dve.tensor_tensor(tiles("XT"), tiles("LT"), wide(K_M1T), ALU.mult).then_inc(x_init, 1)
                dve.wait_ge(x_init, nth(n, 4, 2))
                dve.tensor_tensor(tiles("XT"), wide(K_ID), tiles("XT"), ALU.subtract).then_inc(x_init, 1)
                dve.wait_ge(vk_ps, nth(n, 2, 0))
                dve.tensor_tensor(tiles("vb"), psum_tiles(B0), over(1), ALU.mult).then_inc(vb_done, 1)
                dve.wait_ge(vk_ps, 2 * n)
                dve.tensor_tensor(tiles("kd"), psum_tiles(B1), over(4), ALU.mult).then_inc(kd_done, 1)

            def level(l, n):
                dve.wait_ge(lx, nth(n, LEVELS, l))
                if l == 0:
                    dve.wait_ge(attnT_ps, n)
                dve.tensor_tensor(tiles("A"), psum_tiles(B0), mask(l + 1), ALU.mult).then_inc(am, 1)
                if l < LEVELS - 1:
                    dve.wait_ge(xa, nth(n, LEVELS - 1, l))
                    if l:
                        dve.wait_ge(xu, nth(n, LEVELS - 1, l - 1))
                    dve.tensor_tensor(T["X"][:, :], T["X"][:, :], B1[:, :], ALU.subtract).then_inc(xu, 1)
                dve.wait_ge(xat, nth(n, LEVELS, l))
                dve.tensor_tensor(T["XT"][:, :], T["XT"][:, :], B2[:, :], ALU.subtract).then_inc(xtu, 1)

            def scan(n):
                for c in range(TT):
                    if c > 0:
                        dve.wait_ge(ks, nth(n, TT - 1, c - 1))
                        dve.scalar_tensor_tensor(out=rr[:, :], in0=BS[:, 0:P], scalar=hp[:, 3, c:c + 1],
                                                 in1=tiles("vb")[:, c, :], op0=ALU.mult, op1=ALU.add).then_inc(rr_done, 1)
                    if c < TT - 1:
                        dve.wait_ge(s_ps, nth(n, TT - 1, c))
                        if c == 0:
                            dve.tensor_copy(st[:, :], BS[:, 2 * P:3 * P]).then_inc(s_done, 1)
                        else:
                            dve.wait_ge(s_done, nth(n, TT - 1, c - 1))
                            dve.scalar_tensor_tensor(out=st[:, :], in0=st[:, :], scalar=hp[:, 5, c:c + 1],
                                                     in1=BS[:, 2 * P:3 * P], op0=ALU.mult, op1=ALU.add).then_inc(s_done, 1)

            def finish(n):
                h = n - 1
                dve.wait_ge(o_root, n)
                dve.reciprocal(T["L"][:, :], T["L"][:, :]).then_inc(o_inv, 1)
                dve.wait_ge(o_inv, n)
                dve.scalar_tensor_tensor(out=T["dm"][:, :], in0=BO[:, :], scalar=nrm[:, 0:1], in1=T["L"][:, :],
                                         op0=ALU.mult, op1=ALU.mult).then_inc(o_nrm, 1)
                dve.wait_ge(o_nrm, n)
                dve.tensor_tensor(mixT[:, bass.ds(h, 1), :].rearrange("p o s -> p (o s)"), T["dm"][:, :],
                                  T["sz"][:, :], ALU.mult).then_inc(o_done, 1)

            def iteration(it, gdn=True, last=False):
                if not last:
                    conv_weights(it)
                if gdn:
                    gdn0(it)
                    gdn1(it)
                if not last:
                    conv(it, 0)
                if gdn:
                    level(0, it)
                    level(1, it)
                for l in range(2, LEVELS):
                    if gdn:
                        level(l, it)
                    if not last:
                        conv(it, 1, [l - 2])
                if gdn:
                    scan(it)
                if not last:
                    conv(it, 2)
                if gdn:
                    finish(it)

            dve.wait_ge(cw_done, 1)
            dve.wait_ge(zero_pad, 5)
            dve.wait_ge(table_zero, 16)
            iteration(0, gdn=False)
            with dve.Fori(1, HEADS) as it:
                iteration(it)
            iteration(HEADS, last=True)

            def attend(m, j):
                u = 2 * m + j
                if j == 0:
                    W(dve, at_ps, 2 * m)
                    dve.tensor_copy(kg[:, :], kdup[:, bass.ds(m, 1), :].rearrange("p o s -> p (o s)"))
                    dve.tensor_copy(vg[:, :, :], vtok[:, :, bass.ds(m * HD, HD)])
                    dve.tensor_copy(sl[:, :, :], attn_small[:, :].rearrange("p (a h) -> p a h", a=2)[:, :, bass.ds(m * 4, 4)]).then_inc(at_small, 1)
                dve.wait_ge(at_small, m + 1)
                W(dve, pt_ps, 4 * u)
                for r in range(2):
                    for tp in range(2):
                        dve.wait_ge(sc_ps, 4 * u + (2 * r + tp + 1))
                        dve.scalar_tensor_tensor(out=sc[:, r, tp, :, :], in0=dist[:, tp:tp + 2, :],
                                                 scalar=sl[:, 0, 2 * j + r:2 * j + r + 1],
                                                 in1=[[B0, B1], [B2, BM]][r][tp][:, :].rearrange("p (a b) -> p a b", a=2),
                                                 op0=ALU.mult, op1=ALU.add).then_inc(sc_b, 1)
                        dve.wait_ge(sc_b, 4 * u + (2 * r + tp + 1))
                        dve.tensor_reduce(att8[:, 0, 4 * r + 2 * tp:4 * r + 2 * tp + 2], sc[:, r, tp, :, :], AX.X, ALU.max).then_inc(mx, 1)
                    dve.wait_ge(mx, 4 * u + (2 * r + 2))
                    dve.tensor_scalar(att8[:, 1, 4 * r:4 * r + 4], att8[:, 0, 4 * r:4 * r + 4],
                                      sl[:, 1, 2 * j + r:2 * j + r + 1], -1.0, ALU.max, ALU.mult).then_inc(nmx, 1)
                dve.wait_ge(pexp, u + 1)
                dve.tensor_tensor(att8[:, 4, :], att8[:, 2, :], att8[:, 3, :], ALU.add).then_inc(inv_sum, 1)
                dve.wait_ge(inv_sum, 2 * u + 1)
                dve.reciprocal(att8[:, 4, :], att8[:, 4, :]).then_inc(inv_sum, 1)
                dve.wait_ge(inv_sum, 2 * u + 2)
                for r in range(2):
                    for tp in range(2):
                        c = 4 * r + 2 * tp
                        dve.tensor_tensor(sc[:, r, tp, :, :], sc[:, r, tp, :, :],
                                          att8[:, 4, c:c + 2].rearrange("p (a o) -> p a o", o=1).broadcast_to([P, 2, 2 * P]),
                                          ALU.mult).then_inc(pn, 1)

            dve.wait_ge(v_tok, 2)
            dve.wait_ge(ld_att, 16)
            attend(0, 0)
            attend(0, 1)
            with dve.Fori(1, 3) as m:
                attend(m, 0)
                attend(m, 1)
            attend(3, 0)
            attend(3, 1)
            for i in range(4):
                dve.wait_ge(mix_hi, i + 1)
                dve.tensor_tensor(mxl[:, 4 * i:4 * i + 4, :], mixT[:, 4 * i:4 * i + 4, :],
                                  mxh[:, 4 * i:4 * i + 4, :].bitcast(F32), ALU.subtract).then_inc(mix_lo, 1)

            dve.wait_ge(ld_h, 16)
            r1v = r1[:, :, :].rearrange("p t (n c) -> p t n c", c=S)

            def sums(nt, t):
                if t < 3:
                    dve.wait_ge(y_ps, 3 * nt + (t + 1))
                else:
                    dve.wait_ge(strip_mm, 4 * nt + (O0 + 4))
                v = r1v[:, t, bass.ds(nt, 1), :].rearrange("p o c -> p (o c)")
                dve.scalar_tensor_tensor(out=v, in0=v, scalar=ALPHA, in1=[B0, B1, B2, BM][t][:, :],
                                         op0=ALU.mult, op1=ALU.add).then_inc(y_out, 1)
                dve.wait_ge(y_out, 4 * nt + (t + 1))
                return dve.bn_stats(bns4[:, t, bass.ds(nt, 1), :].rearrange("p o c -> p (o c)"), v)

            with dve.Fori(0, 3) as nt:
                for t in range(TT):
                    sums(nt, t)
            n_l1 = [0]

            def l1_(i):
                n_l1[0] += 1
                i.then_inc(l1_step, 1)
                dve.wait_ge(l1_step, n_l1[0])

            def l1_shift(t):
                dve.wait_ge(l1_root, t + 1)
                l1_(dve.reciprocal(rs4[:, t:t + 1], rs4[:, t:t + 1]))
                l1_(dve.scalar_tensor_tensor(out=nm4[:, t:t + 1], in0=mv4[:, t, 0:1], scalar=-1.0, in1=rs4[:, t:t + 1],
                                             op0=ALU.mult, op1=ALU.mult))
                assert n_l1[0] == l1_bias(t)

            for t in range(TT):
                l1_(sums(3, t))
                l1_(dve.bn_aggr(mv4[:, t, :], bns4[:, t, :, :].rearrange("p a b -> p (a b)")))
                assert n_l1[0] == l1_var(t)
                if t:
                    l1_shift(t - 1)
            l1_shift(TT - 1)
            dve.wait_ge(ld_ln1, 80)
            for t in range(TT - 1):
                dve.wait_ge(l1_norm, t + 1)
                dve.tensor_tensor(r1[:, t, :], r1[:, t, :], g1[:, :], ALU.mult).then_inc(l1_gain, 1)
                dve.wait_ge(l1_gain, t + 1)
                dve.tensor_tensor(r1[:, t, :], r1[:, t, :], b1[:, :], ALU.add).then_inc(h1_done, 1)

            k_ = [0]

            def step(i):
                k_[0] += 1
                i.then_inc(rt, 1)
                dve.wait_ge(rt, k_[0])

            def per(ap, width):
                return ap.rearrange("p (t o) -> p t o", o=1).broadcast_to([P, TT, width])

            def over_t(c0, c1):
                return rc[:, c0:c1].rearrange("p (o e) -> p o e", o=1).broadcast_to([P, TT, c1 - c0])

            dve.wait_ge(logits, 2)
            dve.wait_ge(h1_done, TT - 1)
            dve.wait_ge(h1_last, 2)
            step(dve.tensor_copy(lg[:, :, :], B2[:, 0:TT * 64].rearrange("p (t n) -> p t n", t=TT)[:, :, 0:GROUPS + E]))
            step(dve.tensor_tensor(lg[:, :, :], lg[:, :, :], BM[:, 0:TT * 64].rearrange("p (t n) -> p t n", t=TT)[:, :, 0:GROUPS + E], ALU.add))
            step(dve.tensor_reduce(gm[:, 0, :], lg[:, :, 0:GROUPS], AX.X, ALU.max))
            step(dve.tensor_tensor(ge[:, :, :], lg[:, :, 0:GROUPS], per(gm[:, 0, :], GROUPS), ALU.subtract))
            assert k_[0] == RT_GE
            step(dve.tensor_tensor(gsel[:, :, 0:GROUPS], lg[:, :, 0:GROUPS], per(gm[:, 0, :], GROUPS), ALU.is_equal))
            step(dve.scalar_tensor_tensor(out=gsel[:, :, 0:GROUPS], in0=gsel[:, :, 0:GROUPS], scalar=-8.0,
                                          in1=over_t(0, GROUPS), op0=ALU.mult, op1=ALU.add))
            step(dve.tensor_reduce(gm[:, 2, :], gsel[:, :, 0:GROUPS], AX.X, ALU.min))
            step(dve.tensor_scalar(gm[:, 2, :], gm[:, 2, :], 8.0, None, ALU.add))
            step(dve.tensor_tensor(gsel[:, :, :], over_t(2 * E, 3 * E), per(gm[:, 2, :], E), ALU.is_equal))
            step(dve.tensor_scalar(gsel[:, :, :], gsel[:, :, :], 1.0, -NEG, ALU.subtract, ALU.mult))
            step(dve.tensor_tensor(el[:, :, :], lg[:, :, GROUPS:], gsel[:, :, :], ALU.add))
            for t in range(TT):
                step(dve.max(top[:, t, :], el[:, t, :]))
                step(dve.max_index(topi[:, t, :], top[:, t, :], el[:, t, :]))
            step(dve.tensor_copy(topf[:, :, :], topi[:, :, 0:2]))
            step(dve.tensor_tensor(wts[:, 0, :], top[:, :, 1:2].rearrange("p t o -> p (t o)"),
                                   top[:, :, 0:1].rearrange("p t o -> p (t o)"), ALU.subtract))
            assert k_[0] == RT_D
            for c in range(2):
                step(dve.tensor_tensor(oh[:, c, :, :], over_t(0, E), topf[:, :, c:c + 1].broadcast_to([P, TT, E]), ALU.is_equal))
            step(dve.tensor_tensor(taken[:, :, :], oh[:, 0, :, :], oh[:, 1, :, :], ALU.add))
            assert k_[0] == RT_M
            dve.wait_ge(rt_exp, 2)
            step(dve.tensor_reduce(gm[:, 1, :], ge[:, :, :], AX.X, ALU.add))
            step(dve.reciprocal(gm[:, 3, :], gm[:, 1, :]))
            step(dve.tensor_scalar(wts[:, 2, :], wts[:, 1, :], 1.0, None, ALU.add))
            step(dve.reciprocal(wts[:, 2, :], wts[:, 2, :]))
            step(dve.tensor_tensor(wts[:, 2, :], wts[:, 2, :], gm[:, 3, :], ALU.mult))
            tok_w = toki[:, :, :, :].bitcast(F32)
            step(dve.tensor_copy(tok_w[:, :, 0:1, 1:2].rearrange("p t c o -> p (t c o)"), wts[:, 2, :]))
            step(dve.tensor_tensor(tok_w[:, :, 1:2, 1:2].rearrange("p t c o -> p (t c o)"), wts[:, 2, :], wts[:, 1, :], ALU.mult))
            dve.wait_ge(rt_ps, 1)
            pv = B1[:, 0:TT * E].rearrange("p (t e) -> p t e", t=TT)
            step(dve.tensor_tensor(el[:, :, :], pv, taken[:, :, :], ALU.subtract))
            step(dve.tensor_tensor(el[:, :, :], el[:, :, :], over_t(E, 2 * E), ALU.add))
            step(dve.tensor_copy(tile_sums[:, :, :], B1[:, TT * E:2 * TT * E].rearrange("p (t e) -> p t e", t=TT)))
            for t in range(1, TT):
                step(dve.tensor_tensor(tile_sums[:, t, :], tile_sums[:, t - 1, :], tile_sums[:, t, :], ALU.add))
            step(dve.tensor_tensor(el[:, 1:, :], el[:, 1:, :], tile_sums[:, 0:TT - 1, :], ALU.add))
            for c in range(2):
                step(dve.tensor_tensor(oh[:, c, :, :], oh[:, c, :, :], el[:, :, :], ALU.mult))
                step(dve.tensor_reduce(dstf[:, :, c:c + 1].rearrange("p t o -> p (t o)"), oh[:, c, :, :], AX.X, ALU.add))
            step(dve.tensor_copy(rd[:, :, :], dstf[:, :, :]))
            step(dve.tensor_copy(toki[:, :, :, 0:1].rearrange("p t c r -> p t (c r)"),
                                 rc[:, 3 * E:].rearrange("p (t o) -> p t o", o=1).broadcast_to([P, TT, 2])))
            assert k_[0] == RT_DEST
            nb, cum, one, cnt = (over_nb[:, i, :] for i in range(4))
            step(dve.tensor_copy(cnt, tile_sums[:, TT - 1, :]))
            step(dve.memset(one, 1.0))
            step(dve.memset(nb, 0.0))
            for b in range(1, CAP // SLOTS):
                step(dve.scalar_tensor_tensor(out=nb, in0=cnt, scalar=float(SLOTS * b), in1=nb, op0=ALU.is_gt, op1=ALU.add))
            step(dve.tensor_tensor_scan(cum, one, nb, 0.0, ALU.mult, ALU.add))
            item = rc[0:1, 0:LEFTOVER]
            item_e = item.rearrange("p (i o) -> p i o", o=1).broadcast_to([1, LEFTOVER, E])
            step(dve.tensor_tensor(ovc[:, :, :], over_nb[0:1, 1:2, :].broadcast_to([1, LEFTOVER, E]), item_e, ALU.is_le))
            step(dve.tensor_reduce(ovf[:, 0, :], ovc[:, :, :], AX.X, ALU.add))
            step(dve.tensor_tensor(ovp[:, :, :], ovc[:, :, :], over_nb[0:1, 0:1, :].broadcast_to([1, LEFTOVER, E]), ALU.mult))
            step(dve.tensor_reduce(ovf[:, 1, :], ovp[:, :, :], AX.X, ALU.add))
            step(dve.tensor_scalar(ovf[:, 0, :], ovf[:, 0, :], float(E - 1), None, ALU.min))
            step(dve.tensor_tensor(ovf[:, 2, :], item, ovf[:, 1, :], ALU.subtract))
            step(dve.tensor_scalar(ovf[:, 2, :], ovf[:, 2, :], 1.0, float(SLOTS), ALU.add, ALU.mult))
            step(dve.scalar_tensor_tensor(out=ovf[:, 2, :], in0=ovf[:, 0, :], scalar=float(CAP), in1=ovf[:, 2, :], op0=ALU.mult, op1=ALU.add))
            step(dve.tensor_scalar(ovf[:, 2, :], ovf[:, 2, :], float(E * CAP - SLOTS), None, ALU.min))
            step(dve.tensor_copy(ovi[:, 0:LEFTOVER], ovf[:, 0, :]))
            step(dve.tensor_copy(ovi[:, LEFTOVER:2 * LEFTOVER], ovf[:, 2, :]))
            step(dve.tensor_copy(ovi[:, 2 * LEFTOVER:], over_nb[0:1, 1, E - 1:E]))
            assert k_[0] == RT_ALL

            def add_rows(n, cs, after=None):
                for c in cs:
                    tt, q = piece(c)
                    dve.wait_ge(comb_ps, 4 * TT * n + (c + 1 - 4 * TT))
                    v = r1[:, tt, q * S:(q + 1) * S]
                    dve.tensor_tensor(v, v, [BS, BO][c % 2][:, :], ALU.add).then_inc(comb_done, 1)
                    if after:
                        after(c)

            def block_dve(t, extra=None):
                dve.wait_ge(xT_ps, 2 * t + 2)
                W(dve, gu_used, 4 * t)
                dve.tensor_copy(xbT[:, 8:16, :], PA[1][:, :].rearrange("p (k n) -> p k n", k=8)).then_inc(xT_d, 1)
                if extra is not None:
                    dve.wait_ge(idx_loaded, 32 * extra + 64)
                elif isinstance(t, int):
                    dve.wait_ge(idx_loaded, 32)
                else:
                    dve.wait_ge(idx_next, t)
                W(dve, yw_done, 4 * t)
                dve.tensor_copy(slot_tw[:, 0:1], idx[:, 0:1])
                dve.tensor_copy(slot_tw[:, 1:2], idx[:, 1:2].bitcast(F32)).then_inc(idx_read, 1)
                if extra is None:
                    dve.wait_ge(scattered, 16 * 2 * TT + 32)
                    dve.wait_ge(table_zeroed, 2)
                    dve.wait_ge(idx_read, t + 1)
                    dve.tensor_copy(idx[:, :], idx_all[:, bass.ds(t + 1, 1), :].rearrange("p e o -> p (e o)")).then_inc(idx_next, 1)
                if not isinstance(t, int):
                    add_rows(t, range(0, BEFORE_HID))
                dve.wait_ge(sg_done, t + 1)
                dve.tensor_tensor(hid[SLOTS:P, :], hid[SLOTS:P, :], B0[SLOTS:P, :], ALU.mult).then_inc(hid_done, 1)
                if not isinstance(t, int):
                    add_rows(t, range(BEFORE_HID, 4 * TT))
                dve.wait_ge(idx_read, t + 1)
                dve.tensor_scalar(place[:, :], tokens[:, :], slot_tw[:, 0:1], None, ALU.is_equal).then_inc(placed_, 1)
                for q in range(4):
                    dve.wait_ge(yw_done, 4 * t + (q + 1))
                    dve.tensor_copy(yhl[:, q, :], yw[:, q, :]).then_inc(yw_hi, 1)
                    dve.wait_ge(yw_hi, 4 * t + (q + 1))
                    dve.tensor_tensor(yhl[SLOTS:P, q, :], yw[SLOTS:P, q, :], yhl[SLOTS:P, q, :].bitcast(F32),
                                      ALU.subtract).then_inc(yw_split, 1)

            block_dve(0)
            dve.wait_ge(scaled, TT)
            with dve.Fori(1, E) as t:
                block_dve(t)
            left = dve.value_load(ovi[0:1, 2 * LEFTOVER:2 * LEFTOVER + 1], min_val=0, max_val=LEFTOVER)
            with dve.If(left > 0):
                with dve.Fori(0, left) as i:
                    block_dve(i + E, extra=i)
            dve.wait_ge(ld_ln2, 32)
            last = dve.snap(left + E)

            def stats(now):
                c = now - 1
                if c < 0:
                    return
                tt, q = piece(c)
                dve.wait_ge(comb_done, 4 * TT * last + (c + 1 - 4 * TT))
                dve.bn_stats(bns4[:, tt, q, :], r1[:, tt, q * S:(q + 1) * S]).then_inc(f_step, 1)

            add_rows(last, range(4 * TT), after=stats)
            stats(4 * TT)
            dve.wait_ge(f_step, 4 * TT)
            for t in range(TT):
                dve.bn_aggr(mv4[:, t, :], bns4[:, t, :, :].rearrange("p a b -> p (a b)")).then_inc(f_step, 1)
            dve.wait_ge(f_step, F_VAR)

            def centre(t):
                dve.scalar_tensor_tensor(out=r1[:, t, :], in0=r1[:, t, :], scalar=mv4[:, t, 0:1], in1=g2[:, :],
                                         op0=ALU.subtract, op1=ALU.mult).then_inc(f_gain, 1)

            centre(0)
            dve.wait_ge(f_root, 1)
            dve.reciprocal(rs4[:, :], rs4[:, :]).then_inc(f_step, 1)
            for t in range(1, TT):
                centre(t)
            dve.wait_ge(f_step, F_VAR + 1)
            for t in DVE_TILES:
                dve.wait_ge(f_gain, t + 1)
                dve.scalar_tensor_tensor(out=r1[:, t, :], in0=r1[:, t, :], scalar=rs4[:, t:t + 1], in1=b2[:, :],
                                         op0=ALU.mult, op1=ALU.add).then_inc(f_done, 1)

        @block.tensor
        def _(pe):
            mm = pe.matmul
            pe.wait_ge(ld_const, 16)
            def k_step(bank, hi_, lo_, rh, rl, first, final):
                mm(bank, lo_, rh, start=first, stop=False)
                mm(bank, hi_, rl, start=False, stop=False)
                return mm(bank, hi_, rh, start=False, stop=final)

            pe.wait_ge(ld_gb, 32)
            pe.transpose(TB[5][:, 0:2 * KD], gb_rows[:, :], cst[0:2 * KD, 0:2 * KD]).then_inc(small_T, 1)

            def h_T(k, t):
                return pe.transpose(TB[k % 6][:, t * P:(t + 1) * P], xt[t][:, k * P:(k + 1) * P], ident)

            def k_steps(s, sl, k0, k1):
                for k in range(k0, k1):
                    if k == 0:
                        pe.wait_ge(strip_lo, s + 1)
                        W(pe, strip_out, s - 1)
                    i = k_step(PA[sl][:, :], whi[sl][:, k, :], wlo[sl][:, k, :], hTh[:, k, :], hTl[:, k, :],
                               k == 0, k == KD - 1)
                    if k == KD - 1:
                        i.then_inc(strip_mm, 1)

            for t in range(TT):
                pe.wait_ge(ln_norm, t + 1)
                for k in range(6):
                    if t == 0 and k == 5:
                        pe.wait_ge(gbT_done, 1)
                    i = h_T(k, t)
                    if t == TT - 1:
                        i.then_inc(hT_psum, 1)
            LAG = 4
            for k in range(6, KD + LAG):
                if k < KD:
                    pe.wait_ge(hv_done, k - 5)
                    for t in range(TT):
                        i = h_T(k, t)
                    i.then_inc(hT_psum, 1)
                for k0 in ([k - LAG] if k > 6 else range(k - LAG + 1)):
                    pe.wait_ge(hT_lo, k0 + 1)
                    k_steps(0, 0, k0, k0 + 1)
            pe.wait_ge(ld_small, 16 * 7)
            pe.transpose(BM[:, 0:CONV * 24], cwraw[:, :], cst[0:CONV * 24, 0:CONV * 24]).then_inc(small_T, 1)
            k_steps(1, 1, 0, KD // 2)
            pe.wait_ge(strip_out, 1)
            for c in range(TT):
                i = pe.transpose(B0[:, c * 2 * HEADS:(c + 1) * 2 * HEADS], bd[0:2 * HEADS, c * P:(c + 1) * P],
                                 cst[0:2 * HEADS, 0:2 * HEADS])
            i.then_inc(small_T, 1)
            k_steps(1, 1, KD // 2, KD)
            k_steps(2, slot(1), 0, KD)
            k_steps(3, slot(2), 0, KD)
            pe.wait_ge(bd_done, BD_G)
            g_all = wk[:, 1, :, :].rearrange("p c h -> p (c h)")
            mm(B0[:, 128:128 + TT * HEADS], tri, g_all, start=True, stop=True)
            mm(B0[:, 256:256 + TT * HEADS], ones, g_all, start=True, stop=True).then_inc(gcum, 1)

            def ch(name, c):
                return T[name][:, c * P:(c + 1) * P]

            def steps(it):
                done = [0]

                def feed(n):
                    for _ in range(n):
                        j, k = divmod(done[0], KD)
                        if j < 4:
                            k_steps(4 * it + 1 + j, slot(j), k, k + 1)
                            done[0] += 1
                return feed

            def gdn(n, feed):
                feed(11)
                for j in range(2):
                    pe.wait_ge(sq_done, nth(n, 2, j))
                    mm([B0, B1][j][:, :], ones, T[["dm", "L"][j]][:, :], start=True, stop=True).then_inc(ss_done, 1)
                pe.wait_ge(gb_ready, n)
                for c in range(TT):
                    i = mm(B2[:, c * P:(c + 1) * P], gb[:, c, :], tri, start=True, stop=True)
                i.then_inc(gc_row, 1)
                feed(13)
                pe.wait_ge(unit, 2 * n)
                for c in range(TT):
                    i = mm(B0[:, c * P:(c + 1) * P], ch("k", c), ch("k", c), start=True, stop=True)
                i.then_inc(gram, 1)
                for c in range(TT):
                    i = mm(B1[:, c * P:(c + 1) * P], ch("q", c), ch("k", c), start=True, stop=True)
                i.then_inc(qk, 1)
                feed(3)
                pe.wait_ge(exp_row, n)
                pe.wait_ge(diff, 4 * n)
                pe.wait_ge(L_done, n)
                for c in range(TT):
                    i = pe.transpose(B2[:, c * P:(c + 1) * P], ch("L", c), ident)
                i.then_inc(LT_ps, 1)
                pe.wait_ge(attn_done, n)
                for c in range(TT):
                    i = pe.transpose(BM[:, c * P:(c + 1) * P], ch("A", c), ident)
                i.then_inc(attnT_ps, 1)
                for c in range(TT):
                    i = pe.transpose(B0[:, c * P:(c + 1) * P], ch("v", c), ident)
                i.then_inc(vk_ps, 1)
                for c in range(TT):
                    i = pe.transpose(B1[:, c * P:(c + 1) * P], ch("k", c), ident)
                i.then_inc(vk_ps, 1)
                feed(4)
                pe.wait_ge(LT_done, n)
                pe.wait_ge(x_init, 4 * n)
                pe.wait_ge(vb_done, n)
                pe.wait_ge(kd_done, n)
                for l in range(LEVELS):
                    if l:
                        pe.wait_ge(xu, nth(n, LEVELS - 1, l - 1))
                    for c in range(TT):
                        i = mm(B0[:, c * P:(c + 1) * P], ch("LT", c), ch("X", c), start=True, stop=True)
                    i.then_inc(lx, 1)
                    feed(2)
                    pe.wait_ge(am, nth(n, LEVELS, l))
                    if l:
                        pe.wait_ge(xtu, nth(n, LEVELS, l - 1))
                    if l < LEVELS - 1:
                        for c in range(TT):
                            i = mm(B1[:, c * P:(c + 1) * P], ch("XT", c), ch("A", c), start=True, stop=True)
                        i.then_inc(xa, 1)
                    for c in range(TT):
                        i = mm(B2[:, c * P:(c + 1) * P], ch("A", c), ch("XT", c), start=True, stop=True)
                    i.then_inc(xat, 1)
                    feed(2)
                pe.wait_ge(attnT_done, n)
                pe.wait_ge(qd_done, n)
                pe.wait_ge(xtu, nth(n, LEVELS, LEVELS - 1))
                for c in range(TT):
                    if c:
                        pe.wait_ge(s_done, nth(n, TT - 1, c - 1))
                        mm(BS[:, 0:P], ch("k", c), st[:, :], start=True, stop=True).then_inc(ks, 1)
                        mm(BO[:, c * P:(c + 1) * P], st[:, :], ch("qd", c), start=True, stop=False)
                        feed(1)
                        pe.wait_ge(rr_done, nth(n, TT - 1, c - 1))
                    mm(BS[:, P:2 * P], ch("XT", c), rr[:, :] if c else ch("vb", c), start=True, stop=True).then_inc(vn_ps, 1)
                    feed(1)
                    pe.wait_ge(vn_done, nth(n, TT, c))
                    if c < TT - 1:
                        mm(BS[:, 2 * P:3 * P], ch("kd", c), vn[:, :], start=True, stop=True).then_inc(s_ps, 1)
                    i = mm(BO[:, c * P:(c + 1) * P], vn[:, :], ch("attnT", c), start=not c, stop=True)
                    feed(1)
                i.then_inc(o_ps, 1)
                feed(2)
                pe.wait_ge(o_sq, n)
                mm(BM[:, :], ones, T["A"][:, :], start=True, stop=True).then_inc(o_ss, 1)

            k_steps(4, slot(3), 0, KD)
            with pe.Fori(1, HEADS) as it:
                feed = steps(it)
                pe.wait_ge(par_done, 1)
                gdn(it, feed)
                feed(4 * KD)
            feed = steps(HEADS)
            gdn(HEADS, feed)
            feed(4 * KD)

            for j in range(2):
                pe.wait_ge(strip_out, Q0 - 1 + j)
                pe.wait_ge(o_done, HEADS)
                for t in range(TT):
                    i = pe.transpose([B0, B1][j][:, t * P:(t + 1) * P], vT[:, j, t * P:(t + 1) * P], ident)
                i.then_inc(v_T, 1)
            for j in range(2):
                k_steps(Q0 + j, slot(j), 0, KD)

            def attend(m, j, feed):
                u = 2 * m + j

                pe.wait_ge(at_small, m + 1)
                pe.wait_ge(strip_out, u + (Q0 + 1))
                W(pe, at_out, u)
                for r in range(2):
                    q0, q1 = HD * r, HD * (r + 1)
                    for tp in range(2):
                        for t in (2 * tp, 2 * tp + 1):
                            i = mm([[B0, B1], [B2, BM]][r][tp][:, (t % 2) * 2 * P:(t % 2 + 1) * 2 * P],
                                   aq[j][q0:q1, t * P:(t + 1) * P], kg[q0:q1, t * P:(t + 2) * P], start=True, stop=True)
                        i.then_inc(sc_ps, 1)
                feed(13)
                for r in range(2):
                    pe.wait_ge(pn, 4 * u + (2 * r + 2))
                    for g in range(2):
                        for t in range(TT):
                            i = pe.transpose([BS, BO, B0, B1][2 * r + g][:, t * P:(t + 1) * P],
                                             sc[:, r, t // 2, t % 2, g * P:(g + 1) * P], ident)
                        i.then_inc(pt_ps, 1)
                feed(2)
                pe.wait_ge(pt, 4 * u + 4)
                for t in range(TT):
                    for g in ((0, 1) if t else (1,)):
                        for r in range(2):
                            i = mm(B2[HD * r:HD * (r + 1), t * P:(t + 1) * P], vg[:, t - 1 + g, :],
                                   pT[:, 2 * r + g, t * P:(t + 1) * P], start=g == 0 or not t, stop=g == 1)
                i.then_inc(at_ps, 1)
                feed(KD)

            def q_feed(m, j):
                done = [0]

                def feed(n):
                    for _ in range(n):
                        if done[0] < KD:
                            k_steps(2 * m + (Q0 + j), slot(j), done[0], done[0] + 1)
                            done[0] += 1
                return feed

            for j in range(2):
                attend(0, j, q_feed(1, j))
            with pe.Fori(2, 4) as m:
                for j in range(2):
                    attend(m - 1, j, q_feed(m, j))
            for j in range(2):
                attend(3, j, lambda n: None)

            def project(nt):
                for kg_ in range(4):
                    sl_ = slot(kg_)
                    wh = whi[sl_][:, :, :].rearrange("p (k a) n -> p k (a n)", k=4)
                    wl = wlo[sl_][:, :, :].rearrange("p (k a) n -> p k (a n)", k=4)
                    pe.wait_ge(strip_lo, 4 * nt + (O0 + 1 + kg_))
                    pe.wait_ge(mix_lo, kg_ + 1)
                    for t in range(TT):
                        if kg_ == 0:
                            W(pe, y_out, 4 * nt + (t - 3))
                        for k in range(4):
                            c = 4 * kg_ + k
                            i = k_step([B0, B1, B2, BM][t][:, :], mxh[:, c, t * P:(t + 1) * P], mxl[:, c, t * P:(t + 1) * P],
                                       wh[:, k, :], wl[:, k, :], c == 0, c == KD - 1)
                        if kg_ == 3 and t < 3:
                            i.then_inc(y_ps, 1)
                    i.then_inc(strip_mm, 1)

            pe.wait_ge(at_out, 8)
            project(0)
            with pe.Fori(1, 4) as nt:
                project(nt)

            def router(t):
                for k in range(KD):
                    if k % 4 == 0:
                        pe.wait_ge(h1T_done, 4 * t + k // 4 + 1)
                    r = SLOTS * (k % 2)
                    i = mm(B0[r:r + GROUPS + E, t * P:(t + 1) * P], wr[:, k, :], h1T[:, k, t * P:(t + 1) * P],
                           start=k < 2, stop=k >= KD - 2)
                return i

            pe.wait_ge(ld_ln1, 80)
            for t in range(TT):
                if t < TT - 1:
                    pe.wait_ge(h1_done, t + 1)
                else:
                    pe.wait_ge(h1_last, 2)
                for b in range(4):
                    W(pe, h1T_done, 4 * (t - 1) + b + 1)
                    for k in range(4):
                        i = pe.transpose([PA[0], PA[1], BS, BO][b][:, k * P:(k + 1) * P],
                                         r1[:, t, (4 * b + k) * P:(4 * b + k + 1) * P], ident)
                    i.then_inc(h1T_ps, 1)
                if t:
                    router(t - 1)
            router(TT - 1).then_inc(logits, 1)
            pe.wait_ge(lgT_done, 1)
            for t in range(TT):
                for r in (0, SLOTS):
                    i = mm([B2, BM][r // SLOTS][:, t * 64:t * 64 + GROUPS + E], lgT[r:r + GROUPS + E, t * P:(t + 1) * P],
                           cst[r:r + GROUPS + E, K_ID + r:K_ID + r + GROUPS + E], start=True, stop=True)
            i.then_inc(logits, 1)
            pe.wait_ge(rt, RT_M)
            all_taken = taken[:, :, :].rearrange("p t e -> p (t e)")
            mm(B1[:, 0:TT * E], tri, all_taken, start=True, stop=True)
            mm(B1[:, TT * E:2 * TT * E], ones, all_taken, start=True, stop=True).then_inc(rt_ps, 1)

            def combine(n, c):
                tt, q = piece(c)
                if c == 0:
                    pe.wait_ge(placed_, n)
                if c % TT == 0:
                    pe.wait_ge(yw_split, 4 * n + (q - 3))
                if c >= 2:
                    pe.wait_ge(comb_done, 4 * TT * n + (c - 1 - 4 * TT))
                mm([BS, BO][c % 2][:, :], place[:, tt * P:(tt + 1) * P], yhl[:, q, :],
                   start=True, stop=True).then_inc(comb_ps, 1)

            def block_pe(t):
                pe.wait_ge(gathered, 16 * t + 16)
                W(pe, xT_a, t)
                W(pe, xT_d, t)
                for g in range(2):
                    for k in range(8):
                        i = mm(PA[g][:, k * SLOTS:(k + 1) * SLOTS], xb[:, (8 * g + k) * P:(8 * g + k + 1) * P],
                               cst[0:SLOTS, 0:SLOTS], start=True, stop=True)
                    i.then_inc(xT_ps, 1)
                if isinstance(t, int):
                    pe.wait_ge(xT_a, t + 1)
                    pe.wait_ge(xT_d, t + 1)
                W(pe, hid_done, t)
                if not isinstance(t, int):
                    combine(t, 0)
                    combine(t, 1)
                    pe.wait_ge(xT_a, t + 1)
                    pe.wait_ge(xT_d, t + 1)
                for kg_ in range(4):
                    pe.wait_ge(gu_loaded[kg_], 32 * t + 32)
                    for k in range(4):
                        c = 4 * kg_ + k
                        for h in range(2):
                            i = mm(B0[SLOTS * h:SLOTS * (h + 1), :], xbT[:, c, :], wpiece[2 * kg_ + h][:, k * F:(k + 1) * F],
                                   start=c == 0, stop=c == KD - 1)
                        if k == 3:
                            i.then_inc(gu_used, 1)
                        if not isinstance(t, int) and 2 <= c < BEFORE_HID:
                            combine(t, c)
                if not isinstance(t, int):
                    combine(t, BEFORE_HID)
                    combine(t, BEFORE_HID + 1)
                W(pe, hidT_done, t)
                pe.wait_ge(hid_done, t + 1)
                for c in range(KF):
                    i = mm(B1[:, c * SLOTS:(c + 1) * SLOTS], hid[SLOTS:P, c * P:(c + 1) * P],
                           cst[SLOTS:P, K_ID + SLOTS:K_ID + P], start=True, stop=True)
                i.then_inc(hT_ps, 1)
                W(pe, yw_done, 4 * t)
                if not isinstance(t, int):
                    for c in range(BEFORE_HID + 2, 4 * TT):
                        combine(t, c)
                pe.wait_ge(hidT_done, t + 1)
                for j in range(2):
                    for c in range(KF):
                        if j == 0:
                            pe.wait_ge(dn_loaded[c], 16 * t + 16)
                        for h in range(2):
                            n0 = (2 * j + h) * F
                            i = mm([B2, BM][j][SLOTS * h:SLOTS * (h + 1), :], hidT[:, c, :], wpiece[8 + c][:, n0:n0 + F],
                                   start=c == 0, stop=c == KF - 1)
                        if j == 1:
                            i.then_inc(dn_used, 1)
                        elif c == KF - 1:
                            i.then_inc(dn_half, 1)

            block_pe(0)
            with pe.Fori(1, E) as t:
                block_pe(t)
            pe.wait_ge(rt, RT_ALL)
            left = pe.value_load(ovi[0:1, 2 * LEFTOVER:2 * LEFTOVER + 1], min_val=0, max_val=LEFTOVER)
            with pe.If(left > 0):
                with pe.Fori(0, left) as i:
                    block_pe(i + E)
            last = pe.snap(left + E)
            for c in range(4 * TT):
                combine(last, c)


_INS = ["x", "ln0_g", "ln0_b", "w_in", "conv_w", "a_log", "dt_bias", "gdn_norm_w", "sinks", "w_o", "ln1_g", "ln1_b",
        "w_route_group", "w_route_expert", "w_gate", "w_up", "w_down", "ln2_g", "ln2_b"]


def kernel(**inputs):
    import concourse.bacc as bacc
    from concourse.bass_utils import run_bass_kernel_spmd

    nc = bacc.Bacc("TRN2", target_bir_lowering=False, num_devices=1)
    given = {name: np.ascontiguousarray(inputs[name]) for name in _INS}
    given |= dict(zip(("consts", "att_consts", "route_consts"), shape_constants()))
    arrays, args = {}, []
    for name, a in given.items():
        arrays[f"in_{name}"] = a
        args.append(nc.dram_tensor(f"in_{name}", a.shape, mybir.dt.from_np(a.dtype), kind="ExternalInput").ap())
    args.append(nc.dram_tensor("out", (1, S, D), F32, kind="ExternalOutput").ap())
    build(nc, *args)
    r = run_bass_kernel_spmd(nc, [arrays], core_ids=[0])
    return r.results[0]["out"]
```
